# Optimizing a Trainium2 kernel written in Bass

```python
import math
import jax
import jax.numpy as jnp
from jax import lax
import numpy as np

D_MODEL = 1024
BATCH = 1
SEQ = 1024
DEPTH = 2
DEC_BATCH = 8
DEC_SEQ = 4
PAST_LEN = 512
PAGE_SIZE = 128

HEAD_DIM = 128
N_MIXERS = 2
DIL_GROUPS = ((128, 1), (512, 4), (2048, 16))
N_GROUPS = len(DIL_GROUPS)
HEADS_PER_GROUP = 4
N_HEADS_A = N_GROUPS * HEADS_PER_GROUP
WIDTH_A_QKV = N_HEADS_A * HEAD_DIM
WIDTH_A_OUT = HEADS_PER_GROUP * HEAD_DIM
N_MEM = 256
MEM_HEADS = 4
WIDTH_MEM = MEM_HEADS * HEAD_DIM
N_HEADS_B = 8
WIDTH_B = N_HEADS_B * HEAD_DIM
CONV_W = 4
CHUNK = 64
BRANCH_A = WIDTH_A_OUT + WIDTH_MEM
BRANCH_B = WIDTH_B + WIDTH_MEM
IN_A = 3 * WIDTH_A_QKV + WIDTH_MEM + BRANCH_A
IN_B = 3 * WIDTH_B + 2 * N_HEADS_B + WIDTH_MEM + BRANCH_B
N_LAYERS_A = (DEPTH + 1) // 2
N_LAYERS_B = DEPTH // 2
N_BUCKETS = 32
MAX_EXACT = N_BUCKETS // 2
MAX_DIST = 2048
EPS = 1e-6
NEG = -1e30
SCALE = HEAD_DIM ** -0.5

kernel_name = 'dilated_swa_gated_delta_hybrid_step'

def rmsnorm(x, w):
    xf = x.astype(jnp.float32)
    y = xf * lax.rsqrt(jnp.mean(xf * xf, axis=-1, keepdims=True) + EPS)
    return (y * w.astype(jnp.float32)).astype(x.dtype)

def l2norm(x):
    return x * lax.rsqrt(jnp.sum(x * x, axis=-1, keepdims=True) + EPS)

def rel_bucket(dist):
    df = jnp.maximum(dist, 1).astype(jnp.float32)
    large = MAX_EXACT + (jnp.log(df / MAX_EXACT) / math.log(MAX_DIST / MAX_EXACT)
                         * (N_BUCKETS - MAX_EXACT)).astype(jnp.int32)
    return jnp.where(dist < MAX_EXACT, dist, jnp.minimum(large, N_BUCKETS - 1))

def mem_attend(q, mk, mv):
    s = jnp.einsum('bthe,bmhe->bhtm', q, mk).astype(jnp.float32) * SCALE
    p = jax.nn.softmax(s, axis=-1).astype(mv.dtype)
    return jnp.einsum('bhtm,bmhe->bthe', p, mv)

def dilated_group_prompt(q, k, v, dil, win, bias_tab):
    B, T, H, hd = q.shape
    nb = win // dil
    span = nb * dil
    Tp = -(-T // span) * span
    nblk = Tp // span
    pad = ((0, 0), (0, Tp - T), (0, 0), (0, 0))
    qb, kb, vb = [jnp.pad(a, pad).reshape(B, nblk, nb, dil, H, hd) for a in (q, k, v)]

    def with_prev(a):
        prev = jnp.pad(a, ((0, 0), (1, 0), (0, 0), (0, 0), (0, 0), (0, 0)))[:, :-1]
        return jnp.concatenate([prev, a], axis=2)

    kk, vv = with_prev(kb), with_prev(vb)
    i = jnp.arange(nb)[:, None]
    j = jnp.arange(2 * nb)[None, :]
    dsub = i + nb - j
    band = (dsub >= 0) & (dsub <= nb)
    blk = jnp.arange(nblk)[:, None, None]
    valid = band[None] & ((blk * nb + j[None] - nb) >= 0)
    bias = bias_tab[rel_bucket(jnp.maximum(dsub, 0) * dil)].astype(jnp.float32)
    s = jnp.einsum('bnirhe,bnjrhe->bnrhij', qb, kk).astype(jnp.float32) * SCALE
    s = s + bias.transpose(2, 0, 1)
    s = jnp.where(valid[None, :, None, None], s, NEG)
    lse = jax.nn.logsumexp(s, axis=-1)
    p = jnp.exp(s - lse[..., None]).astype(v.dtype)
    o = jnp.einsum('bnrhij,bnjrhe->bnirhe', p, vv).reshape(B, Tp, H, hd)[:, :T]
    lse = lse.transpose(0, 1, 4, 2, 3).reshape(B, Tp, H)[:, :T]
    return o, lse

def dilated_group_sample(q, k, v, kbuf, vbuf, dil, win, bias_tab):
    B, T, H, hd = q.shape
    L = kbuf.shape[1]
    kc = jnp.concatenate([kbuf, k], axis=1)
    vc = jnp.concatenate([vbuf, v], axis=1)
    nk = win // dil + 1
    jd = jnp.arange(nk) * dil
    pos = PAST_LEN + jnp.arange(T)[:, None] - jd[None]
    idx = pos - (PAST_LEN - L)
    valid = (pos >= 0) & (idx >= 0)
    idx = jnp.clip(idx, 0, L + T - 1)
    kg = kc[:, idx]
    vg = vc[:, idx]
    bias = bias_tab[rel_bucket(jd)].astype(jnp.float32)
    s = jnp.einsum('bthe,btjhe->bthj', q, kg).astype(jnp.float32) * SCALE + bias.T
    s = jnp.where(valid[None, :, None, :], s, NEG)
    lse = jax.nn.logsumexp(s, axis=-1)
    p = jnp.exp(s - lse[..., None]).astype(v.dtype)
    o = jnp.einsum('bthj,btjhe->bthe', p, vg)
    keep = min(win, L + T)
    return o, lse, kc[:, L + T - keep:], vc[:, L + T - keep:]

def layer_a(h, mem_k, mem_v, w_in, w_out, rel_bias, bufs):
    B, T, _ = h.shape
    proj = h @ w_in
    q, k, v, qm, z = jnp.split(proj, [WIDTH_A_QKV, 2 * WIDTH_A_QKV, 3 * WIDTH_A_QKV,
                                      3 * WIDTH_A_QKV + WIDTH_MEM], axis=-1)
    q, k, v = [a.reshape(B, T, N_GROUPS, HEADS_PER_GROUP, HEAD_DIM) for a in (q, k, v)]
    outs, lses, new_bufs = [], [], []
    for g, (win, dil) in enumerate(DIL_GROUPS):
        bias_g = rel_bias[:, g * HEADS_PER_GROUP:(g + 1) * HEADS_PER_GROUP]
        if bufs is None:
            o, l = dilated_group_prompt(q[:, :, g], k[:, :, g], v[:, :, g], dil, win, bias_g)
            keep = min(win, T)
            nkb, nvb = k[:, T - keep:, g], v[:, T - keep:, g]
        else:
            o, l, nkb, nvb = dilated_group_sample(q[:, :, g], k[:, :, g], v[:, :, g],
                                                  bufs[2 * g], bufs[2 * g + 1], dil, win, bias_g)
        outs.append(o)
        lses.append(l)
        new_bufs.extend([nkb, nvb])
    alpha = jax.nn.softmax(jnp.stack(lses, axis=0), axis=0)
    o = jnp.einsum('gbth,gbthe->bthe', alpha.astype(h.dtype), jnp.stack(outs, axis=0))
    om = mem_attend(qm.reshape(B, T, MEM_HEADS, HEAD_DIM), mem_k, mem_v)
    branch = jnp.concatenate([o.reshape(B, T, WIDTH_A_OUT), om.reshape(B, T, WIDTH_MEM)], axis=-1)
    return (branch * jax.nn.silu(z)) @ w_out, new_bufs

def to_chunks(a, C, N):
    B, T = a.shape[:2]
    a = jnp.pad(a, [(0, 0), (0, N * C - T)] + [(0, 0)] * (a.ndim - 2))
    a = a.reshape((B, N, C) + a.shape[2:])
    return a.transpose((1, 0, 3, 2) + tuple(range(4, a.ndim)))

def gated_delta(q, k, v, g, beta, S0):
    B, T, H, dk = q.shape
    dv = v.shape[-1]
    C = min(CHUNK, T)
    N = -(-T // C)
    qc, kc, vc = to_chunks(q, C, N), to_chunks(k, C, N), to_chunks(v, C, N)
    gc = jnp.cumsum(to_chunks(g, C, N), axis=-1)
    bc = to_chunks(beta, C, N)
    tri = jnp.tril(jnp.ones((C, C), dtype=bool))
    strict = jnp.tril(jnp.ones((C, C), dtype=bool), -1)
    diff = gc[..., :, None] - gc[..., None, :]
    decay = jnp.where(tri, jnp.exp(jnp.where(tri, diff, 0.0)), 0.0)
    kb = kc * bc[..., None]
    lmat = jnp.where(strict, jnp.einsum('nbhik,nbhjk->nbhij', kb, kc) * decay, 0.0)
    rhs = jnp.concatenate([vc * bc[..., None], kb * jnp.exp(gc)[..., None]], axis=-1)
    sol = lax.linalg.triangular_solve(lmat, rhs, left_side=True, lower=True, unit_diagonal=True)
    u, w = sol[..., :dv], sol[..., dv:]
    aqk = jnp.einsum('nbhik,nbhjk->nbhij', qc, kc) * decay
    qg = qc * jnp.exp(gc)[..., None]
    g_last = gc[..., -1]
    kdec = kc * jnp.exp(g_last[..., None] - gc)[..., None]

    def step(S, xs):
        u_i, w_i, aqk_i, qg_i, kdec_i, gl_i = xs
        v_new = u_i - jnp.einsum('bhck,bhkv->bhcv', w_i, S)
        o_i = jnp.einsum('bhck,bhkv->bhcv', qg_i, S) + jnp.einsum('bhij,bhjv->bhiv', aqk_i, v_new)
        S = S * jnp.exp(gl_i)[..., None, None] + jnp.einsum('bhck,bhcv->bhkv', kdec_i, v_new)
        return S, o_i

    S, o = lax.scan(step, S0, (u, w, aqk, qg, kdec, g_last))
    o = o.transpose(1, 0, 3, 2, 4).reshape(B, N * C, H, dv)[:, :T]
    return o, S

def layer_b(h, mem_k, mem_v, w_in, conv_w, a_log, dt_bias, o_norm_w, w_out, conv_state, delta_state):
    B, T, _ = h.shape
    proj = h @ w_in
    qkv, b, a, qm, z = jnp.split(proj, [3 * WIDTH_B, 3 * WIDTH_B + N_HEADS_B,
                                        3 * WIDTH_B + 2 * N_HEADS_B,
                                        3 * WIDTH_B + 2 * N_HEADS_B + WIDTH_MEM], axis=-1)
    if conv_state is None:
        prefix = jnp.zeros((B, CONV_W - 1, 3 * WIDTH_B), qkv.dtype)
    else:
        prefix = conv_state.astype(qkv.dtype)
    xpad = jnp.concatenate([prefix, qkv], axis=1)
    conv = xpad[:, 0:T] * conv_w[0]
    for wi in range(1, CONV_W):
        conv = conv + xpad[:, wi:wi + T] * conv_w[wi]
    new_conv = xpad[:, T:]
    conv = jax.nn.silu(conv).astype(jnp.float32)
    q, k, v = [c.reshape(B, T, N_HEADS_B, HEAD_DIM) for c in jnp.split(conv, 3, axis=-1)]
    q = l2norm(q) * SCALE
    k = l2norm(k)
    beta = jax.nn.sigmoid(b.astype(jnp.float32))
    g = -jnp.exp(a_log.astype(jnp.float32)) * jax.nn.softplus(a.astype(jnp.float32)
                                                              + dt_bias.astype(jnp.float32))
    if delta_state is None:
        S0 = jnp.zeros((B, N_HEADS_B, HEAD_DIM, HEAD_DIM), jnp.float32)
        sdt = h.dtype
    else:
        S0 = delta_state.astype(jnp.float32)
        sdt = delta_state.dtype
    o, S = gated_delta(q, k, v, g, beta, S0)
    o = rmsnorm(o, o_norm_w).astype(h.dtype).reshape(B, T, WIDTH_B)
    om = mem_attend(qm.reshape(B, T, MEM_HEADS, HEAD_DIM), mem_k, mem_v).reshape(B, T, WIDTH_MEM)
    branch = jnp.concatenate([o, om], axis=-1) * jax.nn.silu(z)
    return branch @ w_out, new_conv, S.astype(sdt)

def setup_inputs(seed: int = 0) -> dict:
    key = jax.random.key(seed)
    ks = iter(jax.random.split(key, 32))

    def nrm(shape, scale):
        return jax.random.normal(next(ks), shape, jnp.float32) * scale

    def win(g):
        return (N_LAYERS_A, DEC_BATCH, min(DIL_GROUPS[g][0], PAST_LEN), HEADS_PER_GROUP, HEAD_DIM)

    mem_shape = (DEPTH, DEC_BATCH, N_MEM, MEM_HEADS, HEAD_DIM)
    dt = jnp.exp(jax.random.uniform(next(ks), (N_LAYERS_B, N_HEADS_B), jnp.float32,
                                    math.log(1e-3), math.log(1e-1)))
    return {
        'x_prompt': nrm((BATCH, SEQ, D_MODEL), 1.0),
        'x_sample': nrm((DEC_BATCH, DEC_SEQ, D_MODEL), 1.0),
        'cache_win_k0': nrm(win(0), 1.0),
        'cache_win_v0': nrm(win(0), 1.0),
        'cache_win_k1': nrm(win(1), 1.0),
        'cache_win_v1': nrm(win(1), 1.0),
        'cache_win_k2': nrm(win(2), 1.0),
        'cache_win_v2': nrm(win(2), 1.0),
        'state_conv': nrm((N_LAYERS_B, DEC_BATCH, CONV_W - 1, 3 * WIDTH_B), 1.0),
        'state_delta': nrm((N_LAYERS_B, DEC_BATCH, N_HEADS_B, HEAD_DIM, HEAD_DIM), 0.1),
        'cache_mem_k': nrm(mem_shape, 1.0),
        'cache_mem_v': nrm(mem_shape, 1.0),
        'mem_prompt': nrm((BATCH, N_MEM, D_MODEL), 1.0),
        'norm_w': 1.0 + nrm((DEPTH, D_MODEL), 0.02),
        'final_norm_w': 1.0 + nrm((D_MODEL,), 0.02),
        'rel_bias': nrm((N_BUCKETS, N_HEADS_A), 0.5),
        'w_in_a': nrm((N_LAYERS_A, D_MODEL, IN_A), D_MODEL ** -0.5),
        'w_out_a': nrm((N_LAYERS_A, BRANCH_A, D_MODEL), BRANCH_A ** -0.5),
        'w_in_b': nrm((N_LAYERS_B, D_MODEL, IN_B), D_MODEL ** -0.5),
        'conv_w': nrm((N_LAYERS_B, CONV_W, 3 * WIDTH_B), CONV_W ** -0.5),
        'a_log': jnp.log(jax.random.uniform(next(ks), (N_LAYERS_B, N_HEADS_B), jnp.float32, 1.0, 16.0)),
        'dt_bias': jnp.log(jnp.expm1(dt)),
        'o_norm_w': 1.0 + nrm((N_LAYERS_B, HEAD_DIM), 0.02),
        'w_out_b': nrm((N_LAYERS_B, BRANCH_B, D_MODEL), BRANCH_B ** -0.5),
        'w_mem_kv': nrm((DEPTH, D_MODEL, 2 * WIDTH_MEM), D_MODEL ** -0.5),
    }

def reference(x_prompt, x_sample, cache_win_k0, cache_win_v0, cache_win_k1, cache_win_v1,
              cache_win_k2, cache_win_v2, state_conv, state_delta, cache_mem_k, cache_mem_v,
              mem_prompt, norm_w, final_norm_w, rel_bias, w_in_a, w_out_a, w_in_b, conv_w,
              a_log, dt_bias, o_norm_w, w_out_b, w_mem_kv):
    xp, xs = x_prompt, x_sample
    Bp = x_prompt.shape[0]
    p_win = [[] for _ in range(2 * N_GROUPS)]
    s_win = [[] for _ in range(2 * N_GROUPS)]
    p_conv, p_delta, s_conv, s_delta, p_mk, p_mv = [], [], [], [], [], []
    for i in range(DEPTH):
        li = i // N_MIXERS
        hp = rmsnorm(xp, norm_w[i])
        hs = rmsnorm(xs, norm_w[i])
        mkv = jnp.einsum('bmd,de->bme', mem_prompt, w_mem_kv[i])
        mk_p = mkv[..., :WIDTH_MEM].reshape(Bp, N_MEM, MEM_HEADS, HEAD_DIM)
        mv_p = mkv[..., WIDTH_MEM:].reshape(Bp, N_MEM, MEM_HEADS, HEAD_DIM)
        p_mk.append(mk_p)
        p_mv.append(mv_p)
        if i % N_MIXERS == 0:
            yp, bp = layer_a(hp, mk_p, mv_p, w_in_a[li], w_out_a[li], rel_bias, None)
            ys, bs = layer_a(hs, cache_mem_k[i], cache_mem_v[i], w_in_a[li], w_out_a[li], rel_bias,
                             (cache_win_k0[li], cache_win_v0[li], cache_win_k1[li],
                              cache_win_v1[li], cache_win_k2[li], cache_win_v2[li]))
            for n in range(2 * N_GROUPS):
                p_win[n].append(bp[n])
                s_win[n].append(bs[n])
        else:
            yp, cp, dp = layer_b(hp, mk_p, mv_p, w_in_b[li], conv_w[li], a_log[li], dt_bias[li],
                                 o_norm_w[li], w_out_b[li], None, None)
            ys, cs, ds = layer_b(hs, cache_mem_k[i], cache_mem_v[i], w_in_b[li], conv_w[li],
                                 a_log[li], dt_bias[li], o_norm_w[li], w_out_b[li],
                                 state_conv[li], state_delta[li])
            p_conv.append(cp)
            p_delta.append(dp)
            s_conv.append(cs)
            s_delta.append(ds)
        xp = xp + yp
        xs = xs + ys
    y_prompt = rmsnorm(xp, final_norm_w)
    y_sample = rmsnorm(xs, final_norm_w)
    return (y_prompt, y_sample,
            jnp.stack(p_win[0]), jnp.stack(p_win[1]), jnp.stack(p_win[2]),
            jnp.stack(p_win[3]), jnp.stack(p_win[4]), jnp.stack(p_win[5]),
            jnp.stack(p_conv), jnp.stack(p_delta), jnp.stack(p_mk), jnp.stack(p_mv),
            jnp.stack(s_win[0]), jnp.stack(s_win[1]), jnp.stack(s_win[2]),
            jnp.stack(s_win[3]), jnp.stack(s_win[4]), jnp.stack(s_win[5]),
            jnp.stack(s_conv), jnp.stack(s_delta))


_drawn_inputs = setup_inputs


def setup_inputs(seed=0):
    import zlib

    import numpy as np

    out = dict(_drawn_inputs(seed))
    spreads = {}
    factors = {}
    for name, (base, spread) in spreads.items():
        noise = np.random.default_rng([zlib.crc32(name.encode()), seed]).standard_normal(out[name].shape)
        drawn = base * np.exp(spread * noise) if base else spread * noise
        out[name] = jnp.asarray(drawn.astype(out[name].dtype))
    for name, factor in factors.items():
        out[name] = (out[name] * factor).astype(out[name].dtype)
    return out
```

```python
import math
from contextlib import ExitStack

import numpy as np
import concourse.bass as bass
from concourse import mybir
from concourse.alu_op_type import AluOpType as ALU

F32 = mybir.dt.float32
ACT = mybir.ActivationFunctionType
AX = mybir.AxisListType.X

P = 128
D = 1024
KD = D // P
SEQ = 1024
NT = SEQ // P
NB, DT = 8, 4
NS = NB * DT
TOK = SEQ + NS
E = 128
H = 4
GROUPS = ((128, 1), (512, 4), (2048, 16))
PAST = 512
QKV_A = 3 * H * E
HB = 8
WB = HB * E
NMEM = 256
CW = 4
NBUCKET = 32
EPS = 1e-6
NEG = -1e30
SCALE = E ** -0.5
OW = E + 2
RING = 4
LEVELS = 7


def rel_bucket(dist):
    dist = np.asarray(dist)
    df = np.maximum(dist, 1).astype(np.float32)
    half = NBUCKET // 2
    large = half + (np.log(df / np.float32(half)) / np.float32(math.log(2048 / half))
                    * np.float32(NBUCKET - half)).astype(np.int32)
    return np.where(dist < half, dist, np.minimum(large, NBUCKET - 1))


def one_hot(dist, valid):
    b = np.where(valid, rel_bucket(np.maximum(dist, 0)), NBUCKET)
    return (np.arange(NBUCKET + 1).reshape((-1,) + (1,) * b.ndim) == b).astype(np.float32)


def shape_constants():
    y = np.arange(3 * P)
    toep = []
    for g, (win, dil) in enumerate(GROUPS):
        n = P if g < 2 else SEQ // GROUPS[2][1]
        d = (2 * P - 1 - y) if g < 2 else (n - 1 - y)
        toep.append(one_hot(d * dil, (d >= 0) & (d <= win // dil)))
    toep = np.stack(toep, 1)
    t = np.arange(DT)[:, None]
    c = np.arange(P)[None]
    cached = [
        one_hot(P + t - c, c >= t),
        one_hot((P - c) * 4 + 0 * t, (c >= 0) & (t >= 0)),
        one_hot((32 - c % 32) * 16 + 0 * t, c // 32 == t),
    ]
    tn = (np.arange(P) % DT)[None]
    new = [one_hot(t - tn, tn <= t), one_hot(0 * (t - tn), tn == t), one_hot(0 * (t - tn), tn == t)]
    samp = np.stack([np.stack([a, b], 1) for a, b in zip(cached, new)], 1)
    j, i = np.arange(P)[:, None], np.arange(P)[None]
    unit = j // DT == i // DT
    mats = [np.eye(P), j <= i, np.ones((P, P)),
            np.where(i >= j, 0, NEG), np.where(i > j, 0, NEG)]
    low = lambda i, j, k: ((i >> k) & 1 == 1) & ((j >> k) + 1 == (i >> k))
    mats += [low(i, j, 0)] + [low(j, i, k) for k in range(1, LEVELS)]
    mats += [unit & (j <= i), unit, np.where(unit & (i >= j), 0, NEG), np.where(unit & (i > j), 0, NEG),
             np.where(unit, 0, NEG)]
    hsel = np.zeros((P, P))
    hsel[:, :H] = np.arange(P)[:, None] // NS == np.arange(H)[None]
    hsel[:, 32:64] = np.arange(P)[:, None] // DT == np.arange(32)[None]
    mats += [hsel]
    mats = np.stack([np.asarray(m, np.float32) for m in mats], 1)
    return {"c_toep": toep.astype(np.float32).reshape(33, -1),
            "c_samp": samp.astype(np.float32).reshape(33, -1),
            "c_mats": mats.reshape(P, -1)}


(M_ID, M_CUM, M_ONE, M_GE, M_GT, M_LEV) = (0, 1, 2, 3, 4, 5)
(M_SCUM, M_SONE, M_SGE, M_SGT, M_SBLK, M_HSEL) = range(M_LEV + LEVELS, M_LEV + LEVELS + 6)
NMATS = M_HSEL + 1


def after(eng, sem, value):
    if not isinstance(value, int) or value > 0:
        eng.wait_ge(sem, value)


class Chain:

    def __init__(self, nc, eng, name):
        self.eng, self.sem, self.n = eng, nc.alloc_semaphore(name), 0

    def __call__(self, ins):
        self.n += 1
        ins.then_inc(self.sem, 1)
        self.eng.wait_ge(self.sem, self.n)


class Ring:

    def __init__(self, nc, tile, block_of):
        self.slots, self.block_of, self.begun = tile, block_of, 0
        self.loaded = [nc.alloc_semaphore(f"weights_loaded{i}") for i in range(RING)]
        self.used = nc.alloc_semaphore("weights_used")

    def load(self, sp, end):
        for b in range(self.begun, end):
            after(sp, self.used, b - RING + 1)
            sp.dma_start(self.slots[:, b % RING, :, :],
                         self.block_of(b).rearrange("(k p) c -> p k c", p=P)).then_inc(self.loaded[b % RING], 16)
        self.begun = max(self.begun, end)

    def wait(self, pe, b):
        pe.wait_ge(self.loaded[b % RING], 16 * (b // RING + 1))


def build(nc, ins, outs):
    (x_prompt, x_sample, ck0, cv0, ck1, cv1, ck2, cv2, state_conv, state_delta, cmk, cmv, mem_prompt,
     norm_w, final_w, rel_bias, w_in_a, w_out_a, w_in_b, conv_w, a_log, dt_bias, o_norm_w, w_out_b,
     w_mem, c_toep, c_samp, c_mats) = ins
    (y_prompt, y_sample, pk0, pv0, pk1, pv1, pk2, pv2, p_conv, p_delta, p_mk, p_mv,
     sk0, sv0, sk1, sv1, sk2, sv2, s_conv, s_delta) = outs
    dram = lambda name, shape: nc.dram_tensor(name, shape, F32, kind="Internal").ap()
    x1 = dram("x1", [TOK, D])
    toep = dram("toep", [3 * H, P, 3 * P])
    sampb = dram("sampb", [H, 6, DT, P])
    part = dram("part", [2, SEQ, OW])

    size = 52900
    sb = nc.alloc_sbuf_tensor("arena", [P, size], F32)
    at = [0]

    def take(*shape, rows=P):
        n = int(np.prod(shape))
        v = sb[0:rows, at[0]:at[0] + n]
        at[0] += n
        assert at[0] <= size, at
        if len(shape) == 2:
            v = v.rearrange("p (a b) -> p a b", b=shape[1])
        elif len(shape) == 3:
            v = v.rearrange("p (a b c) -> p a b c", b=shape[1], c=shape[2])
        return v

    mats = take(NMATS, P)
    mat = lambda m: mats[:, m, :]
    ident = mat(M_ID)
    hT_at = at[0]
    hT = take(KD, TOK)
    brT = take(12, TOK)

    NMB = 16
    B0 = NMB
    NSTAGE = 4 * H
    B1 = B0 + 3 * NSTAGE
    B2 = B1 + 3 * HB

    def block_cols(s, i):
        h, g = s // 4, s % 4
        if g < 3:
            c = i * QKV_A + g * H * E + h * E
        else:
            c = 3 * QKV_A + (0, H * E, 2 * H * E)[i] + h * E
        return w_in_a[0][:, c:c + P]

    def gate_cols(s, i):
        c = 3 * WB + 2 * HB
        c += (s * P, H * E + (HB + s) * P, H * E + 2 * s * P, H * E + (2 * s + 1) * P)[i]
        return w_in_b[0][:, c:c + P]

    def weight_block(b):
        if b < B0:
            return w_mem[b // 8][:, (b % 8) * P:(b % 8 + 1) * P]
        if b < B1:
            return block_cols((b - B0) // 3, (b - B0) % 3)
        if b < B2:
            c = (b - B1) % 3 * WB + (b - B1) // 3 * P
            return w_in_b[0][:, c:c + P]
        return gate_cols((b - B2) // 4, (b - B2) % 4)

    ring = Ring(nc, take(RING, KD, P), weight_block)
    mkT = take(2 * H, NMEM)
    mv = take(4, H * E)
    qs_at = at[0]
    qs, ks, vs = take(3, P), take(3, P), take(3, P)
    qms = take(P)
    zs = take(12, NS)
    bias_s = take(6, P)
    stat = take(64)
    epsc = take(1)
    rbase = at[0]

    bank = [nc.alloc_psum_tensor(f"bank{i}", [P, 512], F32) for i in range(8)]
    copies = nc.alloc_semaphore("copies")
    stored = {n: nc.alloc_semaphore(f"stored_{n}") for n in (
        "mem", "kv", "new_rows", "state", "conv", "sample_states0", "sample_states1", "y0", "y1")}
    w_out_in = [nc.alloc_semaphore(f"w_out_in{l}") for l in range(2)]
    phase_sems = []

    def sem(name):
        phase_sems.append(nc.alloc_semaphore(name))
        return phase_sems[-1]

    def phase_over():
        nc.clear_and_free_semaphores(list(phase_sems))
        phase_sems.clear()
        nc.all_engine_barrier()

    at[0] = rbase
    qkv = take(2, 3, TOK)
    vtok, ktok = take(NT, P), take(NT, P)
    sS, pr, pT = take(2, 256), take(2, 256), take(2, 256)
    b01 = take(2 * H, 256)
    b2 = take(H, P)
    ocomb = take(NT, P)
    wcomb = take(4, 3 * NT)
    og = [brT[:, 8 + g, 0:NT * OW].rearrange("p (a b) -> p a b", b=OW) for g in range(3)]
    ow = brT[:, 11, 0:NT * OW].rearrange("p (a b) -> p a b", b=OW)
    tabs_in = brT[0:33, 4:8, :].rearrange("p a b -> p (a b)")
    c_tp, c_sp = tabs_in[:, 0:9 * P], tabs_in[:, 9 * P:33 * P]
    relx = brT[0:33, 8, 0:12]
    tr_t = take(9, P)[0:H]
    tr_s = take(24, P)[0:H]

    const_in, tab_in = nc.alloc_semaphore("const_in"), nc.alloc_semaphore("tab_in")
    NTAB = 3 + H * NB

    def copy_cache(pool, src, dst, n, drop):
        for b in range(0, NB, 2):
            pool.dma_start(dst[0, b:b + 2, 0:n - drop].rearrange("b t h e -> b (t h e)"),
                           src[0, b:b + 2, drop:n].rearrange("b t h e -> b (t h e)")).then_inc(copies, 16)
    NCOPY = 6 * NB // 2

    def norm_phase(tag, base, tiles, load, weight, dest):
        at[0] = base
        xs, xn, wb, junk = take(3, D), take(2, D), take(D), take(D)
        loaded = [sem(f"{tag}x_loaded{i}") for i in range(3)]
        eps_set = sem(f"{tag}eps_set")
        w_in, sq, root, normed, tr, ev_a, ev_v = (sem(f"{tag}{n}") for n in (
            "w_in", "sq", "root", "normed", "tr", "ev_a", "ev_v"))
        N = len(tiles)
        nn = [sum(t[1] for t in tiles[:n + 1]) for n in range(N)]
        src = lambda n: xn[:, n % 2] if tiles[n][1] else xs[:, n % 3]
        with nc.Block() as block:
            @block.sync
            def _(sp):
                sp.dma_start(mats[:, 0:1, :], c_mats[:, 0:P].rearrange("p (m c) -> p m c", c=P)).then_inc(w_in, 16)
                sp.dma_start(wb, weight.unsqueeze(0).to_broadcast([P, D])).then_inc(w_in, 16)
                for n, (rows, _) in enumerate(tiles):
                    after(sp, tr, 2 * (n - 2))
                    sp.dma_start(xs[0:rows, n % 3], load(n)).then_inc(loaded[n % 3], 16)
                ring.load(sp, 2)
                sp.dma_start(mats[:, 1:, :], c_mats[:, P:].rearrange("p (m c) -> p m c", c=P)).then_inc(const_in, 16)
                sp.dma_start(c_tp, c_toep).then_inc(const_in, 16)
                sp.dma_start(c_sp, c_samp).then_inc(const_in, 16)
                ring.load(sp, RING)

            @block.scalar
            def _(act):
                def evacuate(n):
                    act.wait_ge(tr, 2 * n + 1)
                    r = tiles[n][0]
                    nc.scalar.copy(dest(n, 0), bank[2 * (n % 2)][:, 0:4 * r].rearrange("p (k r) -> p k r", r=r)
                                   ).then_inc(ev_a, 1)
                act.wait_ge(eps_set, 1)
                for n, (rows, norm) in enumerate(tiles):
                    if norm:
                        act.wait_ge(loaded[n % 3], 16 * (n // 3 + 1))
                        nc.scalar.activation(junk[0:rows], xs[0:rows, n % 3], ACT.Square,
                                             accum_out=stat[0:rows, n:n + 1]).then_inc(sq, 1)
                        act.wait_ge(sq, nn[n])
                        nc.scalar.activation(stat[0:rows, 16 + n:17 + n], stat[0:rows, n:n + 1], ACT.Sqrt,
                                             scale=1.0 / D, bias=epsc[0:rows]).then_inc(root, 1)
                    if n:
                        evacuate(n - 1)
                evacuate(N - 1)

            @block.vector
            def _(dve):
                own = Chain(nc, dve, f"{tag}dve")
                nc.vector.memset(epsc, EPS).then_inc(eps_set, 1)

                def evacuate(n):
                    dve.wait_ge(tr, 2 * n + 2)
                    r = tiles[n][0]
                    nc.vector.tensor_copy(dest(n, 4), bank[2 * (n % 2) + 1][:, 0:4 * r]
                                          .rearrange("p (k r) -> p k r", r=r)).then_inc(ev_v, 1)
                dve.wait_ge(w_in, 32)
                for n, (rows, norm) in enumerate(tiles):
                    if norm:
                        dve.wait_ge(root, nn[n])
                        own(nc.vector.reciprocal(stat[0:rows, 32 + n:33 + n], stat[0:rows, 16 + n:17 + n]))
                        after(dve, tr, 2 * (n - 1))
                        nc.vector.scalar_tensor_tensor(out=xn[0:rows, n % 2], in0=xs[0:rows, n % 3],
                                                       scalar=stat[0:rows, 32 + n:33 + n], in1=wb[0:rows],
                                                       op0=ALU.mult, op1=ALU.mult).then_inc(normed, 1)
                    if n:
                        evacuate(n - 1)
                evacuate(N - 1)

            @block.tensor
            def _(pe):
                pe.wait_ge(w_in, 32)
                for n, (rows, norm) in enumerate(tiles):
                    if norm:
                        pe.wait_ge(normed, nn[n])
                    else:
                        pe.wait_ge(loaded[n % 3], 16 * (n // 3 + 1))
                    after(pe, ev_a, n - 1)
                    after(pe, ev_v, n - 1)
                    for k in range(KD):
                        i = nc.tensor.transpose(bank[2 * (n % 2) + k // 4][:, (k % 4) * rows:(k % 4 + 1) * rows],
                                                src(n)[0:rows, k * P:(k + 1) * P], ident[0:rows, 0:rows])
                        if k % 4 == 3:
                            i.then_inc(tr, 1)

    def tok_cols(n):
        return slice(n * P, min((n + 1) * P, TOK))

    memT = brT[:, 0:2, 0:KD * P].rearrange("p c (k r) -> p k c r", r=P)

    def dest_in(n, k):
        return hT[:, k:k + 4, tok_cols(n)] if n <= NT else memT[:, k:k + 4, n - NT - 1, :]

    def load_in(n):
        if n < NT:
            return x_prompt[0, n * P:(n + 1) * P]
        if n == NT:
            return x_sample.rearrange("b t d -> (b t) d")
        return mem_prompt[0, (n - NT - 1) * P:(n - NT) * P]

    norm_phase("in_", rbase, [(P, 1)] * NT + [(NS, 1), (P, 0), (P, 0)], load_in, norm_w[0], dest_in)

    phase_over()

    at[0] = rbase
    vT_m, mk_tok = take(2, NMEM), take(4, H * E)
    mem_ev, mem_tr, mem_tev = (sem(n) for n in ("mem_ev", "mem_tr", "mem_tev"))
    mem_out = stored["mem"]
    rel_in, rel_set, tab_mm, tab_row, tab_out, b2_set = (sem(n) for n in (
        "rel_in", "rel_set", "table_mm", "table_row", "table_out", "b2_set"))

    def table_rows_out(sp):
        sp.wait_ge(tab_row, 9)
        for g in range(3):
            sp.dma_start(toep[g * H:(g + 1) * H],
                         tr_t[:, 3 * g:3 * g + 3, :].rearrange("h a b -> h (a b)").unsqueeze(1)
                         .to_broadcast([H, P, 3 * P])).then_inc(tab_out, 16)
        sp.dma_start(sampb.rearrange("h g t c -> h (g t) c"), tr_s).then_inc(tab_out, 16)

    def tables_in(sp):
        sp.wait_ge(tab_out, 64)
        sp.wait_ge(b2_set, 1)
        sp.dma_start(b01[:, :, :], bass.AP(toep.tensor, P - 1, [[3 * P - 1, P], [P * 3 * P, 2 * H], [1, 256]])
                     ).then_inc(tab_in, 16)
        for r in range(2):
            sp.dma_start(b2[64 * r:64 * r + 64, :, 64 * r:64 * r + 64],
                         bass.AP(toep.tensor, 2 * H * P * 3 * P + 63,
                                 [[3 * P - 1, 64], [P * 3 * P, H], [1, 64]])).then_inc(tab_in, 16)
        for h in range(H):
            for b in range(NB):
                sp.dma_start(bias_s[h * NS + b * DT:h * NS + (b + 1) * DT],
                             sampb[h].rearrange("g t c -> t g c")).then_inc(tab_in, 16)

    with nc.Block() as block:
        @block.sync
        def _(sp):
            sp.wait_ge(rel_set, 1)
            sp.dma_start(relx[0:NBUCKET, :], rel_bias).then_inc(rel_in, 16)
            table_rows_out(sp)
            ring.load(sp, 2 * RING)
            tables_in(sp)
            ring.load(sp, NMB + RING)
            for l in range(2):
                sp.wait_ge(mem_tev, 8 * (l + 1))
                for dst, src in ((p_mk, mk_tok), (p_mv, mv)):
                    sp.dma_start(dst[l, 0].rearrange("(c p) h e -> p c (h e)", p=P),
                                 src[:, 2 * l:2 * l + 2, :]).then_inc(mem_out, 16)
            sp.wait_ge(mem_out, 64)

        @block.tensor
        def _(pe):
            def turn(b):
                pe.wait_ge(mem_ev, b + 1)
                after(pe, mem_tev, b - 1)
                src = mkT[:, (b // 8) * H + b % 4, :] if b % 8 < 4 else vT_m[:, b % 2]
                for c in range(2):
                    i = nc.tensor.transpose(bank[2 + b % 2][:, c * P:(c + 1) * P], src[:, c * P:(c + 1) * P], ident)
                i.then_inc(mem_tr, 1)

            def tables():
                pe.wait_ge(const_in, 48)
                pe.wait_ge(rel_in, 16)
                for m in range(9):
                    g = m if m < 3 else (m - 3) // 2
                    rhs = c_tp[:, m * 3 * P:(m + 1) * 3 * P] if m < 3 else c_sp[:, (m - 3) * 512:(m - 2) * 512]
                    after(pe, tab_row, m - 3)
                    nc.tensor.matmul(bank[4 + m % 4][0:H, 0:rhs.shape[1]], relx[:, g * H:(g + 1) * H], rhs,
                                     start=True, stop=True).then_inc(tab_mm, 1)
            for b in range(NMB):
                if b == 2:
                    tables()
                ring.wait(pe, b)
                after(pe, mem_ev, b - 1)
                for k in range(KD):
                    i = nc.tensor.matmul(bank[b % 2][:, 0:NMEM], ring.slots[:, b % RING, k, :],
                                         memT[:, k, :, :], start=k == 0, stop=k == KD - 1)
                i.then_inc(ring.used, 1)
                if b:
                    turn(b - 1)
            turn(NMB - 1)

        @block.scalar
        def _(act):
            for b in range(NMB):
                act.wait_ge(ring.used, b + 1)
                if b % 8 >= 4:
                    after(act, mem_tr, b - 1)
                dst = mkT[:, (b // 8) * H + b % 4, :] if b % 8 < 4 else vT_m[:, b % 2]
                nc.scalar.copy(dst, bank[b % 2][:, 0:NMEM]).then_inc(mem_ev, 1)

        @block.vector
        def _(dve):
            nc.vector.memset(relx, NEG).then_inc(rel_set, 1)
            nc.vector.memset(b2[:, :, :], NEG).then_inc(b2_set, 1)
            for m in range(9):
                dve.wait_ge(tab_mm, m + 1)
                n = 3 * P if m < 3 else 512
                dst = tr_t[:, 3 * m:3 * m + 3, :] if m < 3 else tr_s[:, 4 * (m - 3):4 * (m - 3) + 4, :]
                nc.vector.tensor_copy(dst.rearrange("h a b -> h (a b)"),
                                      bank[4 + m % 4][0:H, 0:n]).then_inc(tab_row, 1)
            for b in range(NMB):
                dve.wait_ge(mem_tr, b + 1)
                dst = (mk_tok if b % 8 < 4 else mv)[:, 2 * (b // 8):2 * (b // 8) + 2, (b % 4) * E:(b % 4 + 1) * E]
                nc.vector.tensor_copy(dst, bank[2 + b % 2][:, 0:NMEM].rearrange("p (c e) -> p c e", e=E)
                                      ).then_inc(mem_tev, 1)

    phase_over()

    ENT = (14, 14, 16, 12)
    EBASE = (0, 14, 28, 44, 56)

    def permuted(v, g, u):
        if g != 1:
            return v[:, u * P:(u + 1) * P]
        o = 512 * (u // 4) + u % 4
        return v[:, o:o + 4 * P - 3:4]

    wide = lambda g, u: g == 3 or (g == 0 and u > 0) or (g == 1 and u >= 4)
    kprev = lambda g, u: u - 1 if g == 0 else u - 4

    (pj_done, pj_read, sc_done, sc_read, mx_done, p_done, p_norm, t_done, t_read, pv_done, o_read,
     og_out, og_in, comb_w, comb_e, comb_o) = (sem(n) for n in (
         "piece_done", "piece_read", "scores_done", "scores_read", "max_done", "probs_done", "probs_normed",
         "turned", "turned_read", "values_done", "values_read",
         "partials_out", "partials_in", "group_weights", "group_exps", "combined"))
    kv_out = stored["kv"]
    sB, tB, oB = (bank[3], bank[4]), (bank[5], bank[6]), bank[7]

    unit = lambda s, u: 8 * s + u

    PARTS = [(j, k) for j in range(1, 9) for k in (range(KD) if j % 3 < 2 else (None,))]
    TURNS = (6, 6, 8, 0)
    FIRST = [max(n - 2, 0) for n in TURNS]

    def parts_beside(g, u):
        cut = lambda x: FIRST[g] + x * (len(PARTS) - FIRST[g]) // 8
        return PARTS[cut(u):cut(u + 1)]

    def ended_beside(g, u):
        return [j for j, k in parts_beside(g, u) if k in (None, KD - 1)]

    with nc.Block() as block:
        @block.sync
        def _(sp):
            ring.load(sp, B0 + 6)
            for s in range(NSTAGE):
                h, g = s // 4, s % 4
                e0 = EBASE[g] + 56 * h
                if g < 3:
                    sp.wait_ge(t_read, e0 + (6, 6, 8)[g])
                    for src, dst in ((ktok, (pk0, pk1, pk2)[g]), (vtok, (pv0, pv1, pv2)[g])):
                        d = dst[0, 0, :, h, :]
                        if g == 0:
                            sp.dma_start(d, src[:, NT - 1, :]).then_inc(kv_out, 16)
                        elif g == 1:
                            sp.dma_start(d.rearrange("(i r) e -> i r e", r=4), src[:, 4:8, :]).then_inc(kv_out, 16)
                        else:
                            for r in range(2):
                                sp.dma_start(d.rearrange("(i a r) e -> r i a e", a=8, r=2)[r],
                                             src[64 * r:64 * r + 64, :, :]).then_inc(kv_out, 16)
                if s + 2 < NSTAGE:
                    ring.load(sp, B0 + 3 * (s + 3))
                if g in (1, 2):
                    sp.wait_ge(o_read, 8 * (s + 1))
                    after(sp, og_in, 16 * 2 * h)
                    if g == 1:
                        pt = part[0].rearrange("(n i r) c -> n i r c", i=P, r=4)
                        for n in range(2):
                            sp.dma_start(pt[n], ow[:, 4 * n:4 * n + 4, :]).then_inc(og_out, 16)
                    else:
                        pt = part[1].rearrange("(i a r) c -> r i a c", a=8, r=2)
                        for r in range(2):
                            sp.dma_start(pt[r], ow[64 * r:64 * r + 64, :, :]).then_inc(og_out, 16)
                    sp.wait_ge(og_out, 16 * (4 * h + 2 * g))
                    after(sp, comb_o, h)
                    sp.dma_start(og[g][:, :, :], part[g - 1].rearrange("(n p) c -> p n c", p=P)).then_inc(og_in, 16)
            sp.wait_ge(kv_out, 16 * 8 * H)

        @block.tensor
        def _(pe):
            def piece(s, j, ks=range(KD)):
                i, part_ = j // 3, j % 3
                b = 3 * s + i
                if ks[0] == 0:
                    if part_ == 0:
                        ring.wait(pe, B0 + b)
                    after(pe, pj_read, 3 * b + part_ - 2)
                for k in ks:
                    rhs = hT[:, k, part_ * 512:(part_ + 1) * 512] if part_ < 2 else hT[:, k, SEQ:TOK]
                    dst = bank[part_][:, 0:rhs.shape[1]]
                    m = nc.tensor.matmul(dst, ring.slots[:, (B0 + b) % RING, k, :], rhs,
                                         start=k == 0, stop=k == KD - 1)
                if ks[-1] == KD - 1:
                    m.then_inc(pj_done if part_ < 2 else ring.used, 1)

            def beside(s, parts):
                if s + 1 < NSTAGE:
                    for j, k in parts:
                        piece(s + 1, j, range(KD) if k is None else (k,))

            def turn(e, pairs):
                after(pe, t_read, e - 1)
                for c, src in pairs:
                    m = nc.tensor.transpose(tB[e % 2][:, c * P:(c + 1) * P], src, ident)
                m.then_inc(t_done, 1)

            def scores(s, u):
                g, x = s % 4, unit(s, u)
                q = permuted(qkv[:, s % 2, 0], g if g < 3 else 0, u)
                after(pe, sc_read, x - 1)
                if g == 3:
                    k, c = mkT[:, s // 4, :], 0
                elif wide(g, u):
                    c = 0
                    o = (u - 1) * P if g == 0 else u % 4
                    k = qkv[:, s % 2, 1, o:o + 256] if g == 0 else qkv[:, s % 2, 1, o:o + 1021:4]
                else:
                    c, k = P, permuted(qkv[:, s % 2, 1], g, u)
                nc.tensor.matmul(sB[x % 2][:, c:256], q, k, start=True, stop=True).then_inc(sc_done, 1)

            def turn_probs(s, u):
                g, x, h = s % 4, unit(s, u), s // 4
                e = EBASE[g] + 56 * h + ENT[g] - (8 if g < 3 else 12) + u
                if g == 3:
                    pe.wait_ge(p_norm, 8 * h + u + 1)
                else:
                    pe.wait_ge(p_done, x + 1)
                cs = (0, 1) if wide(g, u) else (1,)
                turn(e, [(c, pr[:, x % 2, c * P:(c + 1) * P]) for c in cs])

            def values(s, u):
                g, x, h = s % 4, unit(s, u), s // 4
                e = EBASE[g] + 56 * h + ENT[g] - (8 if g < 3 else 12) + u
                cs = (0, 1) if wide(g, u) else (1,)
                pe.wait_ge(t_read, e + 1)
                after(pe, o_read, x)
                for c in cs:
                    w = pT[:, x % 2, c * P:(c + 1) * P]
                    if g == 3:
                        m = nc.tensor.matmul(oB[:, 0:P], mv[:, c, h * E:(h + 1) * E], w,
                                             start=c == cs[0], stop=c == 1)
                    else:
                        m = nc.tensor.matmul(oB[:, 0:P], w, vtok[:, kprev(g, u) if c == 0 else u, :],
                                             start=c == cs[0], stop=c == 1)
                m.then_inc(pv_done, 1)

            for j in range(9):
                piece(0, j)
            piece(1, 0)
            for s in range(NSTAGE):
                h, g = s // 4, s % 4
                pe.wait_ge(pj_read, 9 * (s + 1))
                if g < 3:
                    e = EBASE[g] + 56 * h
                    for t in range(4):
                        beside(s, PARTS[max(t - 2, 0):max(t - 1, 0)])
                        turn(e + t, [(c, permuted(qkv[:, s % 2, 2], g, 2 * t + c)) for c in range(2)])
                    for t, us in enumerate(((6, 7), (4, 5)) if g == 0 else ((4, 5), (6, 7)) if g == 1 else
                                           ((0, 1), (2, 3), (4, 5), (6, 7))):
                        beside(s, PARTS[t + 2:t + 3])
                        turn(e + 4 + t, [(c, permuted(qkv[:, s % 2, 1], g, us[c])) for c in range(2)])
                for u in range(8):
                    scores(s, u)
                    if u:
                        turn_probs(s, u - 1)
                    beside(s, parts_beside(g, u))
                    if u:
                        values(s, u - 1)
                turn_probs(s, 7)
                if s + 2 < NSTAGE:
                    piece(s + 2, 0)
                values(s, 7)
                if g == 3:
                    pe.wait_ge(comb_o, h + 1)
                    for t in range(4):
                        turn(EBASE[3] + 56 * h + 8 + t, [(c, ocomb[:, 2 * t + c, :]) for c in range(2)])

        @block.scalar
        def _(act):
            def piece(s, j):
                i, part_ = j // 3, j % 3
                b, h, g = 3 * s + i, s // 4, s % 4
                if j == 0:
                    after(act, o_read, 8 * (s - 1))
                    if g == 1:
                        after(act, t_read, EBASE[4] * h)
                if part_ < 2:
                    act.wait_ge(pj_done, 2 * b + part_ + 1)
                    src, dst = bank[part_][:, :], qkv[:, s % 2, i, part_ * 512:(part_ + 1) * 512]
                    if g == 2:
                        src = src.rearrange("e (i r) -> e i r", r=16)
                        dst = qkv[:, s % 2, i, 0:SEQ].rearrange("e (r i) -> e i r", r=16)[:, 32 * part_:32 * part_ + 32]
                else:
                    act.wait_ge(ring.used, B0 + b + 1)
                    src = bank[2][:, 0:NS]
                    if g < 3:
                        dst = (qs, ks, vs)[i][:, g, h * NS:(h + 1) * NS]
                    else:
                        dst = (qms[:, h * NS:(h + 1) * NS], zs[:, h, :], zs[:, H + h, :])[i]
                nc.scalar.activation(dst, src, ACT.Silu if g == 3 and i else ACT.Copy).then_inc(pj_read, 1)

            def exps(s, u):
                g, x = s % 4, unit(s, u)
                c = 0 if wide(g, u) else P
                act.wait_ge(mx_done, x + 1)
                if g == 3:
                    nm, l = stat[:, u:u + 1], stat[:, 8 + u:9 + u]
                    after(act, p_norm, 8 * (s // 4) + u - 7)
                else:
                    o = ow if g else og[0]
                    nm, l = o[:, u, E:E + 1], o[:, u, E + 1:E + 2]
                nc.scalar.activation(pr[:, x % 2, c:256], sS[:, x % 2, c:256], ACT.Exp, bias=nm,
                                     accum_out=l).then_inc(p_done, 1)

            for j in range(9):
                piece(0, j)
            for s in range(NSTAGE):
                more = s + 1 < NSTAGE
                if more:
                    piece(s + 1, 0)
                for u in range(8):
                    if unit(s, u) >= 2:
                        act.wait_ge(pv_done, unit(s, u) - 1)
                    exps(s, u)
                    if s % 4 == 3 and u == 4:
                        act.wait_ge(comb_w, s // 4 * 2 + 1)
                        nc.scalar.activation(wcomb[:, 1, :], wcomb[:, 0, :], ACT.Exp).then_inc(comb_e, 1)
                    if more:
                        for j in ended_beside(s % 4, u):
                            piece(s + 1, j)

        @block.vector
        def _(dve):
            own = Chain(nc, dve, "dve_a")
            dve.wait_ge(tab_in, 16 * NTAB)
            for g in range(3):
                own(nc.vector.tensor_tensor(bias_s[:, 2 * g + 1, :], bias_s[:, 2 * g + 1, :], mat(M_SBLK), ALU.add))

            def turned(e, dst, w=256, lo=0):
                dve.wait_ge(t_done, e + 1)
                nc.vector.tensor_copy(dst, tB[e % 2][:, lo:lo + w]).then_inc(t_read, 1)

            def top(s, u):
                g, x, h = s % 4, unit(s, u), s // 4
                c = 0 if wide(g, u) else P
                dve.wait_ge(sc_done, x + 1)
                after(dve, p_done, x - 1)
                if g == 3:
                    i = nc.vector.tensor_scalar(sS[:, x % 2, :], sB[x % 2][:, 0:256], SCALE, None, ALU.mult)
                else:
                    bias = b2[:, h, :] if g == 2 else b01[:, g * H + h, c:256]
                    i = nc.vector.scalar_tensor_tensor(out=sS[:, x % 2, c:256], in0=sB[x % 2][:, c:256], scalar=SCALE,
                                                       in1=bias, op0=ALU.mult, op1=ALU.add)
                i.then_inc(sc_read, 1)
                dve.wait_ge(sc_read, x + 1)
                nm = stat[:, u:u + 1] if g == 3 else (ow if g else og[0])[:, u, E:E + 1]
                nc.vector.reduce_max(nm, sS[:, x % 2, c:256], axis=AX, negate=True).then_inc(mx_done, 1)

            def normed(s, u):
                g, x, h = s % 4, unit(s, u), s // 4
                if g == 3:
                    dve.wait_ge(p_done, x + 1)
                    own(nc.vector.reciprocal(stat[:, 16 + u:17 + u], stat[:, 8 + u:9 + u]))
                    nc.vector.tensor_scalar(pr[:, x % 2, :], pr[:, x % 2, :], stat[:, 16 + u:17 + u], None,
                                            ALU.mult).then_inc(p_norm, 1)

            def probs_turned(s, u):
                g, x, h = s % 4, unit(s, u), s // 4
                e = EBASE[g] + 56 * h + ENT[g] - (8 if g < 3 else 12) + u
                c = 0 if wide(g, u) else P
                turned(e, pT[:, x % 2, c:256], 256 - c, c)

            def outputs(s, u):
                g, x, h = s % 4, unit(s, u), s // 4
                dve.wait_ge(pv_done, x + 1)
                if g == 3:
                    i = nc.vector.tensor_tensor(brT[:, H + h, u * P:(u + 1) * P], oB[:, 0:P],
                                                qkv[:, s % 2, 2, u * P:(u + 1) * P], ALU.mult)
                else:
                    i = nc.vector.tensor_copy((ow if g else og[0])[:, u, 0:E], oB[:, 0:P])
                i.then_inc(o_read, 1)

            def weights(h):
                dve.wait_ge(og_in, 16 * 2 * (h + 1))
                nm = [og[g][:, :, E] for g in range(3)]
                l = [og[g][:, :, E + 1] for g in range(3)]
                e = [wcomb[:, 1, g * NT:(g + 1) * NT] for g in range(3)]
                m, r = wcomb[:, 3, 0:NT], wcomb[:, 3, NT:2 * NT]
                own(nc.vector.tensor_tensor(m, nm[0], nm[1], ALU.min))
                own(nc.vector.tensor_tensor(m, m, nm[2], ALU.min))
                for g in range(3):
                    i = nc.vector.tensor_tensor(wcomb[:, 0, g * NT:(g + 1) * NT], m, nm[g], ALU.subtract)
                i.then_inc(comb_w, 1)
                dve.wait_ge(comb_e, h + 1)
                for g in range(3):
                    own(nc.vector.tensor_tensor(wcomb[:, 2, g * NT:(g + 1) * NT], e[g], l[g], ALU.mult))
                own(nc.vector.tensor_tensor(r, wcomb[:, 2, 0:NT], wcomb[:, 2, NT:2 * NT], ALU.add))
                own(nc.vector.tensor_tensor(r, r, wcomb[:, 2, 2 * NT:3 * NT], ALU.add))
                own(nc.vector.reciprocal(m, r))
                for g in range(3):
                    i = nc.vector.tensor_tensor(wcomb[:, 2, g * NT:(g + 1) * NT], e[g], m, ALU.mult)
                i.then_inc(comb_w, 1)

            for s in range(NSTAGE):
                h, g = s // 4, s % 4
                e = EBASE[g] + 56 * h
                if g < 3:
                    after(dve, kv_out, 16 * (8 * h + (0, 2, 4)[g]))
                    for t in range(4):
                        turned(e + t, vtok[:, 2 * t:2 * t + 2, :])
                    for t, u in enumerate(((6, 4) if g == 0 else (4, 6) if g == 1 else (0, 2, 4, 6))):
                        turned(e + 4 + t, ktok[:, u:u + 2, :])
                if g == 2:
                    dve.wait_ge(og_out, 16 * (4 * h + 2))
                if g == 1:
                    after(dve, og_out, 16 * 4 * h)
                for u in range(8):
                    top(s, u)
                    if u:
                        probs_turned(s, u - 1)
                    normed(s, u)
                    if u:
                        outputs(s, u - 1)
                    if g == 3 and u == 4:
                        weights(h)
                probs_turned(s, 7)
                outputs(s, 7)
                if g == 3:
                    for t in range(4):
                        e = EBASE[3] + 56 * h + 8 + t
                        dve.wait_ge(t_done, e + 1)
                        nc.vector.tensor_tensor(brT[:, h, t * 256:(t + 1) * 256], tB[e % 2][:, 0:256],
                                                qkv[:, s % 2, 1, t * 256:(t + 1) * 256], ALU.mult).then_inc(t_read, 1)

        @block.gpsimd
        def _(pool):
            own = Chain(nc, pool, "pool_a")
            for h in range(H):
                copy_cache(pool, *((ck1, sk1, 512, DT), (cv1, sv1, 512, DT), (ck0, sk0, 128, DT),
                                   (cv0, sv0, 128, DT))[h])
                pool.wait_ge(comb_w, 2 * h + 2)
                after(pool, t_read, EBASE[4] * h)
                w = lambda g: wcomb[:, 2, g * NT:(g + 1) * NT].unsqueeze(2).to_broadcast([P, NT, E])
                own(nc.gpsimd.tensor_tensor(ocomb[:, :, :], og[0][:, :, 0:E], w(0), ALU.mult))
                own(nc.gpsimd.tensor_tensor(og[1][:, :, 0:E], og[1][:, :, 0:E], w(1), ALU.mult))
                own(nc.gpsimd.tensor_tensor(og[2][:, :, 0:E], og[2][:, :, 0:E], w(2), ALU.mult))
                own(nc.gpsimd.tensor_tensor(ocomb[:, :, :], ocomb[:, :, :], og[1][:, :, 0:E], ALU.add))
                nc.gpsimd.tensor_tensor(ocomb[:, :, :], ocomb[:, :, :], og[2][:, :, 0:E], ALU.add).then_inc(comb_o, 1)

    phase_over()

    def sample_attention(tag, kcache, vcache, nset, q_of, bias, out_of, new, base, ahead=None):
        at[0] = base
        NC = 6
        N = NB * len(kcache)
        kc = take(NC, 512)
        kT = take(2, 512)
        st = take(nset, P)
        nparts = 2 if new else 1
        W = nset * nparts
        S, pt_ = take(W, P), take(W, P)
        osum = take(P)
        kn, vn = (take(3, P), take(3, P)) if new else (None, None)
        m = take(4)
        ld = [sem(f"{tag}cache_loaded{i}") for i in range(NC)]
        (ktd, kta, ktv, std, stc, srow, smx, sexp, sn, ptd, ptv, nd, nev, vd, od, ob) = (
            sem(f"{tag}{n}") for n in ("keys_turned", "keys_read_act", "keys_read_dve", "scores", "scores_copied",
                                       "rows", "max", "exp", "softmax", "probs_turned",
                                       "probs_read_dve", "new_turned", "new_read", "values_used", "values_done",
                                       "summed"))
        outd = stored["new_rows"]
        tile_of = lambda i: (i // len(kcache), i % len(kcache))

        def cols(h, b, ts):
            o = h * NS + b * DT
            return slice(o, o + DT) if ts is None else slice(o + ts, o + ts + 1)

        with nc.Block() as block:
            @block.sync
            def _(sp):
                for j in range(2 * N):
                    b, c = tile_of(j % N)
                    src, _, _ = (kcache if j < N else vcache)[c]
                    if j >= NC:
                        k = j - NC
                        if k < N:
                            sp.wait_ge(ktd, k + 1)
                        else:
                            sp.wait_ge(vd, k - N + 1)
                    sp.dma_start(kc[:, j % NC, :], src(b)).then_inc(ld[j % NC], 16)
                    i = j // NC - 1
                    if ahead and j % NC == 0 and 0 <= i < ahead[0] // 4:
                        sp.dma_start(sb[:, rbase + 4 * i * D:rbase + 4 * (i + 1) * D].rearrange("p (k c) -> p k c", c=D),
                                     ahead[1][512 * i:512 * (i + 1)].rearrange("(k p) c -> p k c", p=P)
                                     ).then_inc(ahead[2], 16)
                if new:
                    sp.wait_ge(nev, 2)
                    for src, dsts in ((kn, (sk0, sk1, sk2)), (vn, (sv0, sv1, sv2))):
                        for g in range(3):
                            n = dsts[g].shape[2]
                            for h in range(H):
                                sp.dma_start(dsts[g][0, :, n - DT:n, h, :], src[h * NS:(h + 1) * NS, g, :]
                                             ).then_inc(outd, 16)
                    sp.wait_ge(outd, 16 * 6 * H)

            @block.tensor
            def _(pe):
                def scores(i):
                    b, c = tile_of(i)
                    _, g, ts = kcache[c]
                    if i % 2:
                        pe.wait_ge(ktv, i // 2 + 1)
                    else:
                        pe.wait_ge(kta, i // 2 + 1)
                    for h in range(H):
                        cs = cols(h, b, ts)
                        x = nc.tensor.matmul(bank[2][:, g * P + cs.start:g * P + cs.stop],
                                             kT[:, i % 2, h * P:(h + 1) * P], q_of(g)[:, cs], start=True, stop=True)
                    x.then_inc(std, 1)
                if new:
                    for n, src in enumerate((ks, vs)):
                        for g in range(3):
                            x = nc.tensor.transpose(bank[5 + n][:, g * P:(g + 1) * P], src[:, g, :], ident)
                        x.then_inc(nd, 1)
                    for g in range(3):
                        x = nc.tensor.matmul(bank[4][:, g * P:(g + 1) * P], qs[:, g, :], ks[:, g, :],
                                             start=True, stop=True)
                    x.then_inc(nd, 1)
                for i in range(N):
                    pe.wait_ge(ld[i % NC], 16 * (i // NC + 1))
                    if i >= 2:
                        if i % 2:
                            pe.wait_ge(ktv, i // 2)
                        else:
                            pe.wait_ge(kta, i // 2)
                    for h in range(H):
                        x = nc.tensor.transpose(bank[i % 2][:, h * P:(h + 1) * P], kc[:, i % NC, h * P:(h + 1) * P],
                                                ident)
                    x.then_inc(ktd, 1)
                    if i:
                        scores(i - 1)
                scores(N - 1)
                pe.wait_ge(stc, 1)
                for g in range(nset):
                    x = nc.tensor.transpose(bank[3][:, g * P:(g + 1) * P], st[:, g, :], ident)
                x.then_inc(srow, 1)
                pe.wait_ge(sn, 1)
                if new:
                    pe.wait_ge(nev, 2)
                for k in range(W):
                    x = nc.tensor.transpose(bank[5 + k // 4][:, (k % 4) * P:(k % 4 + 1) * P], S[:, k, :], ident)
                x.then_inc(ptd, 1)
                pe.wait_ge(ptv, 1 + (W > 4))
                for i in range(N):
                    b, c = tile_of(i)
                    _, g, ts = vcache[c]
                    j = N + i
                    pe.wait_ge(ld[j % NC], 16 * (j // NC + 1))
                    for h in range(H):
                        cs = cols(h, b, ts)
                        x = nc.tensor.matmul(bank[7][:, g * P + cs.start:g * P + cs.stop],
                                             kc[:, j % NC, h * P:(h + 1) * P], pt_[:, g * nparts, cs],
                                             start=True, stop=True)
                    x.then_inc(vd, 1)
                if new:
                    for g in range(3):
                        x = nc.tensor.matmul(bank[7][:, 3 * P:4 * P], vn[:, g, :], pt_[:, 2 * g + 1, :],
                                             start=g == 0, stop=g == 2)
                    x.then_inc(od, 1)

            @block.scalar
            def _(act):
                for i in range(0, N, 2):
                    act.wait_ge(ktd, i + 1)
                    if i >= 2:
                        act.wait_ge(std, i - 1)
                    nc.scalar.copy(kT[:, 0, :], bank[0][:, :]).then_inc(kta, 1)
                act.wait_ge(smx, 1)
                nc.scalar.activation(S[:, :, :].rearrange("p a b -> p (a b)"), S[:, :, :].rearrange("p a b -> p (a b)"),
                                     ACT.Exp, bias=m[:, 0:1], scale=1.0, accum_out=m[:, 1:2]).then_inc(sexp, 1)

            @block.vector
            def _(dve):
                own = Chain(nc, dve, f"{tag}dve")
                if new:
                    for n, dst in enumerate((kn, vn)):
                        dve.wait_ge(nd, n + 1)
                        nc.vector.tensor_copy(dst[:, :, :].rearrange("p a b -> p (a b)"),
                                              bank[5 + n][:, 0:3 * P]).then_inc(nev, 1)
                for i in range(1, N, 2):
                    dve.wait_ge(ktd, i + 1)
                    if i >= 2:
                        dve.wait_ge(std, i - 1)
                    nc.vector.tensor_copy(kT[:, 1, :], bank[1][:, :]).then_inc(ktv, 1)
                dve.wait_ge(std, N)
                nc.vector.tensor_copy(st[:, :, :].rearrange("p a b -> p (a b)"), bank[2][:, 0:nset * P]
                                      ).then_inc(stc, 1)
                dve.wait_ge(srow, 1)
                rows = lambda b: b[:, 0:nset * P].rearrange("p (g c) -> p g c", c=P)
                if bias is None:
                    own(nc.vector.tensor_scalar(S[:, :, :], rows(bank[3]), SCALE, None, ALU.mult))
                else:
                    dve.wait_ge(nd, 3)
                    for k in range(2):
                        own(nc.vector.scalar_tensor_tensor(
                            out=S[:, k:W:2, :], in0=rows(bank[3 + k]), scalar=SCALE,
                            in1=bias[:, k:W:2, :], op0=ALU.mult, op1=ALU.add))
                nc.vector.reduce_max(m[:, 0:1], S[:, :, :].rearrange("p a b -> p (a b)"), axis=AX,
                                     negate=True).then_inc(smx, 1)
                dve.wait_ge(sexp, 1)
                own(nc.vector.reciprocal(m[:, 2:3], m[:, 1:2]))
                nc.vector.tensor_scalar(S[:, :, :], S[:, :, :], m[:, 2:3], None, ALU.mult).then_inc(sn, 1)
                dve.wait_ge(ptd, 1)
                for k in range(0, W, 4):
                    n = min(4, W - k)
                    nc.vector.tensor_copy(pt_[:, k:k + n, :].rearrange("p a b -> p (a b)"),
                                          bank[5 + k // 4][:, 0:n * P]).then_inc(ptv, 1)
                dve.wait_ge(vd, N)
                if new:
                    dve.wait_ge(od, 1)
                own(nc.vector.tensor_copy(osum, bank[7][:, 0:P]))
                for k in range(1, nset + (1 if new else 0)):
                    own(nc.vector.tensor_tensor(osum, osum, bank[7][:, k * P:(k + 1) * P], ALU.add))
                nc.vector.tensor_tensor(brT[:, out_of:out_of + H, SEQ:TOK],
                                        osum.rearrange("p (h t) -> p h t", h=H),
                                        zs[:, out_of:out_of + H, :], ALU.mult).then_inc(ob, 1)

        phase_over()

    def win_sources(c0, c1, c2):
        flat = lambda a: (lambda b: a[0, b].rearrange("t h e -> t (h e)"))
        f0, f1, f2 = flat(c0), flat(c1), flat(c2)
        tiles = [(f0, 0, None)]
        for t in range(DT):
            tiles.append((lambda b, t=t: f1(b)[t:PAST - 3 + t:4], 1, t))
        tiles.append((lambda b: f2(b).rearrange("(c r) e -> r c e", r=16)[0:DT], 2, None))
        return tiles

    def mem_sources(c, l):
        return [(lambda b, k=k: c[l, b, k * P:(k + 1) * P].rearrange("t h e -> t (h e)"), k, None) for k in range(2)]

    sample_attention("sw_", win_sources(ck0, ck1, ck2), win_sources(cv0, cv1, cv2), 3, lambda g: qs[:, g, :],
                     bias_s, 0, True, rbase)
    sample_attention("sm0_", mem_sources(cmk, 0), mem_sources(cmv, 0), 2, lambda g: qms, None, H, False,
                     rbase + 8 * D, (8, w_out_a[0], w_out_in[0]))

    def out_phase(tag, nblk, w_loaded, x_of, weight, base, last):
        at[0] = rbase
        wo = take(nblk, D)
        at[0] = base
        xs, xo, wb, junk = take(2, D), take(2, D), take(D), take(D)
        NX = NT + 1
        rows = lambda n: P if n < NT else NS
        ld = [sem(f"{tag}x_loaded{i}") for i in range(2)]
        (w_in, yd, ya, sq, root, nm, tr, eva, evv, xout) = (sem(f"{tag}{n}") for n in (
            "norm_w_in", "y_done", "y_added", "squared", "root", "normed", "turned", "read_act", "read_dve",
            "stream_out"))
        yo = (stored["y0"], stored["y1"])

        def store(sp, n):
            if last:
                sp.wait_ge(nm, n + 1)
                dst = y_prompt[0, n * P:(n + 1) * P] if n < NT else y_sample.rearrange("b t d -> (b t) d")
                sp.dma_start(dst, xo[0:rows(n), n % 2]).then_inc(yo[n % 2], 16)
            else:
                sp.wait_ge(ya, 2 * (n + 1))
                sp.dma_start(x1[n * P:n * P + rows(n)], xs[0:rows(n), n % 2]).then_inc(xout, 16)

        with nc.Block() as block:
            @block.sync
            def _(sp):
                sp.dma_start(wb, weight.unsqueeze(0).to_broadcast([P, D])).then_inc(w_in, 16)
                for n in range(NX):
                    if n >= 2:
                        sp.wait_ge(nm, n - 1)
                        if not last:
                            sp.wait_ge(xout, 16 * (n - 1))
                    sp.dma_start(xs[0:rows(n), n % 2], x_of(n)).then_inc(ld[n % 2], 16)
                    if n:
                        store(sp, n - 1)
                store(sp, NX - 1)
                if last:
                    sp.wait_ge(yo[0], 16 * ((NX + 1) // 2))
                    sp.wait_ge(yo[1], 16 * (NX // 2))
                else:
                    sp.wait_ge(xout, 16 * NX)

            @block.tensor
            def _(pe):
                pe.wait_ge(w_loaded, 16 * (nblk // 4))
                for n in range(NX + 1):
                    if n < NX:
                        for half in range(2):
                            after(pe, ya, 2 * n + half - 1)
                            for k in range(nblk):
                                i = nc.tensor.matmul(bank[half][0:rows(n), :], brT[:, k, n * P:n * P + rows(n)],
                                                     wo[:, k, half * 512:(half + 1) * 512],
                                                     start=k == 0, stop=k == nblk - 1)
                            i.then_inc(yd, 1)
                    if n and not last:
                        m = n - 1
                        r = rows(m)
                        pe.wait_ge(nm, m + 1)
                        after(pe, eva, m - 1)
                        after(pe, evv, m - 1)
                        for k in range(KD):
                            i = nc.tensor.transpose(bank[2 + 2 * (m % 2) + k // 4][:, (k % 4) * r:(k % 4 + 1) * r],
                                                    xo[0:r, m % 2, k * P:(k + 1) * P], ident[0:r, 0:r])
                            if k % 4 == 3:
                                i.then_inc(tr, 1)

            @block.scalar
            def _(act):
                def evacuate(n):
                    act.wait_ge(tr, 2 * n + 1)
                    r = rows(n)
                    nc.scalar.copy(hT[:, 0:4, tok_cols(n)], bank[2 + 2 * (n % 2)][:, 0:4 * r]
                                   .rearrange("p (k r) -> p k r", r=r)).then_inc(eva, 1)
                for n in range(NX):
                    r = rows(n)
                    act.wait_ge(ya, 2 * (n + 1))
                    nc.scalar.activation(junk[0:r], xs[0:r, n % 2], ACT.Square,
                                         accum_out=stat[0:r, n:n + 1]).then_inc(sq, 1)
                    act.wait_ge(sq, n + 1)
                    nc.scalar.activation(stat[0:r, 16 + n:17 + n], stat[0:r, n:n + 1], ACT.Sqrt,
                                         scale=1.0 / D, bias=epsc[0:r]).then_inc(root, 1)
                    if n and not last:
                        evacuate(n - 1)
                if not last:
                    evacuate(NX - 1)

            @block.vector
            def _(dve):
                own = Chain(nc, dve, f"{tag}dve")

                def evacuate(n):
                    dve.wait_ge(tr, 2 * n + 2)
                    r = rows(n)
                    nc.vector.tensor_copy(hT[:, 4:8, tok_cols(n)], bank[3 + 2 * (n % 2)][:, 0:4 * r]
                                          .rearrange("p (k r) -> p k r", r=r)).then_inc(evv, 1)
                dve.wait_ge(w_in, 16)
                for n in range(NX):
                    r = rows(n)
                    dve.wait_ge(ld[n % 2], 16 * (n // 2 + 1))
                    for half in range(2):
                        dve.wait_ge(yd, 2 * n + half + 1)
                        c = slice(half * 512, (half + 1) * 512)
                        nc.vector.tensor_tensor(xs[0:r, n % 2, c], bank[half][0:r, :], xs[0:r, n % 2, c],
                                                ALU.add).then_inc(ya, 1)
                    dve.wait_ge(root, n + 1)
                    own(nc.vector.reciprocal(stat[0:r, 32 + n:33 + n], stat[0:r, 16 + n:17 + n]))
                    if n >= 2 and last:
                        dve.wait_ge(yo[n % 2], 16 * (n // 2))
                    elif n >= 2:
                        dve.wait_ge(tr, 2 * (n - 1))
                    nc.vector.scalar_tensor_tensor(out=xo[0:r, n % 2], in0=xs[0:r, n % 2],
                                                   scalar=stat[0:r, 32 + n:33 + n], in1=wb[0:r],
                                                   op0=ALU.mult, op1=ALU.mult).then_inc(nm, 1)
                    if n and not last:
                        evacuate(n - 1)
                if not last:
                    evacuate(NX - 1)

        phase_over()

    def x0_of(n):
        return x_prompt[0, n * P:(n + 1) * P] if n < NT else x_sample.rearrange("b t d -> (b t) d")

    out_phase("oa_", 8, w_out_in[0], x0_of, norm_w[1], rbase + 8 * D, False)

    at[0] = rbase
    xpad = take(3, SEQ + CW - 1)
    xpad_s = take(3, NB * (CW - 1 + DT))
    qkvT = take(2, 3, SEQ)
    LT, AT, M, MT, X = (take(NT, P) for _ in range(5))
    o_sb = take(NT, P)
    t1, r_sb, vn = take(2, P), take(2, P), take(2, P)
    S = take(2, P)
    cst = take(24, NB * (CW - 1))
    cwT = take(CW, 24)
    NG = 66
    beta, lbeta, g_, gc, gl, eg, egl, ekd = (take(NG) for _ in range(8))
    eglu = take(64)
    onw = take(1)
    hd = take(2, 8, NT)
    kdec = mkT[:, 0:H, :].rearrange("p a b -> p (a b)").rearrange("p (c e) -> p c e", e=P)
    vb = mv[:, 0:2, :].rearrange("p a b -> p (a b)").rearrange("p (c e) -> p c e", e=P)
    flat = lambda v: v.rearrange("p a b -> p (a b)")
    nconv = sb[:, qs_at:qs_at + 24 * 27].rearrange("p (b r) -> p b r", r=27)
    sd = flat(bias_s).rearrange("p (i t) -> p i t", i=3)

    hrep = qkvT[:, 0, 0, :].rearrange("p (k t) -> p k t", t=P)
    crow = qkvT[0:24, 1, :, :].rearrange("p a b -> p (a b)")[:, 0:3 * WB]
    wrow = qkvT[0:96, 0, 1, 0:P]
    wba = qkvT[:, 0, 1, P:2 * P].rearrange("p (k c) -> p k c", c=16)
    ad = qkvT[:, 0, 1, 400:416].rearrange("p (a c) -> p a c", a=2)
    gt = [qkvT[:, 0, 2, 144 * i:144 * (i + 1)].rearrange("p (n c) -> p n c", c=2 * HB) for i in range(6)]
    sel = qkvT[:, 0, 1, 432:448].rearrange("p (a b) -> p a b", b=H)
    unit_g = qkvT[:, 0, 1, 448:512]

    gin, hrd, gmm, gev, ge, gm2, cmm = (sem(f"gate_{n}") for n in ("in", "rep", "mm", "read", "act", "sums", "conv"))
    with nc.Block() as block:
        @block.sync
        def _(sp):
            sp.dma_start(wba, w_in_b[0][:, 3 * WB:3 * WB + 2 * HB].rearrange("(k p) c -> p k c", p=P)).then_inc(gin, 16)
            sp.dma_start(ad[:, 0, :], a_log.to_broadcast([P, HB])).then_inc(gin, 16)
            sp.dma_start(ad[:, 1, :], dt_bias.to_broadcast([P, HB])).then_inc(gin, 16)
            sp.dma_start(wrow, conv_w[0].rearrange("w (b p) -> (w b) p", p=P)).then_inc(gin, 16)
            sp.dma_start(crow, state_conv[0].rearrange("b w c -> (b w) c")).then_inc(gin, 16)
            with nc.allow_non_contiguous_dma(reason="128 words, once"):
                sp.dma_start(onw, o_norm_w.rearrange("a e -> e a")).then_inc(gin, 16)
            ring.load(sp, B1 + RING)

        @block.tensor
        def _(pe):
            pe.wait_ge(gin, 96)
            pe.wait_ge(hrd, 1)
            for n in range(NT + 1):
                for k in range(KD):
                    l = hT[:, k, n * P:(n + 1) * P] if n < NT else hrep[:, k, :]
                    i = nc.tensor.matmul(bank[0][:, 16 * n:16 * n + 16], l, wba[:, k, :], start=k == 0, stop=k == KD - 1)
            i.then_inc(gmm, 1)
            nc.tensor.transpose(bank[1][:, 0:96], wrow, ident[0:96, 0:96]).then_inc(cmm, 1)
            for b in range(24):
                i = nc.tensor.transpose(bank[2 + b // 12][:, (b % 12) * 24:(b % 12 + 1) * 24],
                                        crow[:, b * P:(b + 1) * P], ident[0:24, 0:24])
            i.then_inc(cmm, 1)
            pe.wait_ge(gev, 2)
            nc.tensor.matmul(bank[4][:, 0:64], mat(M_CUM), g_[:, 0:64], start=True, stop=True)
            nc.tensor.matmul(bank[4][:, 64:66], mat(M_SCUM), g_[:, 64:66], start=True, stop=True)
            nc.tensor.matmul(bank[5][:, 0:64], mat(M_ONE), g_[:, 0:64], start=True, stop=True)
            nc.tensor.matmul(bank[5][:, 64:66], mat(M_SONE), g_[:, 64:66], start=True, stop=True)
            nc.tensor.matmul(bank[5][:, 66:130], mat(M_ONE), unit_g, start=True, stop=True).then_inc(gm2, 1)

        @block.scalar
        def _(act):
            act.wait_ge(gin, 96)
            nc.scalar.activation(ad[:, 0, :], ad[:, 0, :], ACT.Exp)
            act.wait_ge(gev, 1)
            nc.scalar.activation(gt[2], gt[1], ACT.Exp, scale=-1.0).then_inc(ge, 1)
            act.wait_ge(ge, 1)
            nc.scalar.activation(gt[3], gt[2], ACT.Ln, bias=1.0).then_inc(ge, 1)
            act.wait_ge(gev, 3)
            nc.scalar.activation(beta, lbeta, ACT.Exp)
            nc.scalar.activation(eg, gc, ACT.Exp)
            nc.scalar.activation(egl, gl, ACT.Exp)
            nc.scalar.activation(eglu, eglu, ACT.Exp)
            nc.scalar.activation(ekd, ekd, ACT.Exp).then_inc(ge, 1)

        @block.vector
        def _(dve):
            own = Chain(nc, dve, "gate_dve")
            for k in range(KD):
                i = nc.vector.tensor_copy(hrep[:, k, :].rearrange("p (r t) -> p r t", r=H),
                                          hT[:, k, SEQ:TOK].unsqueeze(1).to_broadcast([P, H, NS]))
            i.then_inc(hrd, 1)
            dve.wait_ge(gin, 96)
            dve.wait_ge(gmm, 1)
            y = gt[0]
            own(nc.vector.tensor_scalar(y[:, :, 0:HB], bank[0][:, 0:144].rearrange("p (n c) -> p n c", c=16)[:, :, 0:HB],
                                        -1.0, None, ALU.mult))
            own(nc.vector.tensor_tensor(y[:, :, HB:2 * HB],
                                        bank[0][:, 0:144].rearrange("p (n c) -> p n c", c=16)[:, :, HB:2 * HB],
                                        ad[:, 1, :].unsqueeze(1).to_broadcast([P, 9, HB]), ALU.add))
            own(nc.vector.tensor_scalar(gt[4], y, -1.0, None, ALU.mult))
            nc.vector.tensor_tensor(gt[1], gt[4], y, ALU.max).then_inc(gev, 1)
            own(nc.vector.tensor_scalar(gt[5], y, 0.0, None, ALU.max))
            dve.wait_ge(ge, 2)
            own(nc.vector.tensor_tensor(gt[5], gt[5], gt[3], ALU.add))
            own(nc.vector.tensor_scalar(ad[:, 0, :], ad[:, 0, :], -1.0, None, ALU.mult))
            own(nc.vector.tensor_tensor(gt[5][:, :, HB:2 * HB], gt[5][:, :, HB:2 * HB],
                                        ad[:, 0, :].unsqueeze(1).to_broadcast([P, 9, HB]), ALU.mult))
            own(nc.vector.tensor_scalar(gt[5][:, :, 0:HB], gt[5][:, :, 0:HB], -1.0, None, ALU.mult))
            for src, dst in ((0, lbeta), (HB, g_)):
                own(nc.vector.tensor_copy(dst[:, 0:64].rearrange("p (n h) -> p n h", h=HB),
                                          gt[5][:, 0:NT, src:src + HB]))
                own(nc.vector.tensor_tensor(sel[:, 0:2, :], gt[5][:, NT, src:src + HB].rearrange("p (a b) -> p a b", b=H),
                                            mats[:, M_HSEL, 0:H].unsqueeze(1).to_broadcast([P, 2, H]), ALU.mult))
                own(nc.vector.reduce_sum(dst[:, 64:66], sel[:, 0:2, :], axis=AX))
            for t in range(2):
                i = nc.vector.tensor_scalar(unit_g[:, 32 * t:32 * t + 32], mats[:, M_HSEL, 32:64],
                                            g_[:, 64 + t:65 + t], None, ALU.mult)
            i.then_inc(gev, 1)
            dve.wait_ge(cmm, 1)
            nc.vector.tensor_copy(flat(cwT), bank[1][:, 0:96])
            dve.wait_ge(cmm, 2)
            for t in range(2):
                own(nc.vector.tensor_copy(flat(cst[:, 12 * t:12 * t + 12, :]), bank[2 + t][:, 0:288]))
            dve.wait_ge(gm2, 1)
            own(nc.vector.tensor_copy(gc, bank[4][:, 0:66]))
            own(nc.vector.tensor_copy(gl, bank[5][:, 0:66]))
            own(nc.vector.tensor_copy(eglu, bank[5][:, 66:130]))
            nc.vector.tensor_tensor(ekd, gl, gc, ALU.subtract).then_inc(gev, 1)

    phase_over()

    GR = ((0, 4), (4, 8))
    NPB = 9
    NWB = 5
    work = []
    for h in range(HB):
        work.append((h, "ss", "act"))
        for gr in range(2):
            work += [(h, f"{n}{gr}", "dve") for n in ("rl", "ra", "kt", "vt", "kk", "qk")]
        work += [(h, "m0", "act"), (h, "m1", "act")]
        for k in range(1, LEVELS):
            work += [(h, f"x{k}{gr}", "dve") for gr in range(2)]
            for gr in range(2):
                work.append((h, f"zt{k}{gr}", "dve"))
                if k < LEVELS - 1:
                    work.append((h, f"z{k}{gr}", "dve"))
        if h:
            work += [(h - 1, "ot0", "dve"), (h - 1, "ot1", "dve")]
        for c in range(NT):
            work += [(h, f"ks{c}", "dve"), (h, f"qs{c}", "act"), (h, f"tr{c}", "act"), (h, f"av{c}", "dve"),
                     (h, f"su{c}", "dve")]
    work += [(HB - 1, "ot0", "dve"), (HB - 1, "ot1", "dve")]
    place, count, read_at = {}, {"act": 0, "dve": 0}, []
    for n, (h, name, who) in enumerate(work):
        count[who] += 1
        place[(h, name)] = n
        read_at.append((who, count[who]))

    (pd, pr_, wk, rd_act, rd_dve, cvd, sild, sqd, hdv, hda, exd, mt0, onm, sqo, fac, tails, prefix, szero, sqrt_o, cstep) = (
        sem(f"b_{n}") for n in (
            "piece_done", "piece_read", "work_done", "work_read_act", "work_read_dve", "convolved", "silu_done",
            "squares_done", "head_dve", "head_act", "exps", "inverse_begun", "outputs_normed", "out_squares",
            "out_factors", "conv_tails", "conv_prefix", "state_zero", "out_roots", "conv_steps"))
    s_out = stored["state"]
    reads = {"act": rd_act, "dve": rd_dve}

    def left(eng, h, name):
        n = place[(h, name)]
        eng.wait_ge(wk, n + 1)
        return bank[3 + n % NWB]

    def readout(eng, h, name):
        who, v = read_at[place[(h, name)]]
        eng.wait_ge(reads[who], v)

    col = lambda c, h: slice(c * HB + h, c * HB + h + 1)
    hcols = lambda v, h: v[:, h:64:HB]
    RQ, RK, LK, NC_, KD_, BI, RW, SO = range(8)
    slots = {"ss": 4, "prep": 4, "m": 1}
    slots.update({f"l{k}{x}": 1 for k in range(1, LEVELS) for x in "ab"})
    for c in range(NT):
        for x, n in zip("abc", (2, 2, 2) if c < 3 else (2, 1, 1) if c < 6 else (0, 0, 0)):
            slots[f"r{c}{x}"] = n
    units = [(j, k) for j in range(NPB) for k in (range(KD) if j % 3 < 2 else (None,))]
    assert sum(slots.values()) == len(units)
    at_slot, begun = {}, 0
    for name, n in slots.items():
        at_slot[name] = units[begun:begun + n]
        begun += n
    ended = {name: [j for j, k in us if k in (None, KD - 1)] for name, us in at_slot.items()}
    conv_at = {0: 0, 1: 0, 3: 1, 4: 1, 6: 2, 7: 2}
    silu_at = {1: 0, 4: 1, 7: 2}

    with nc.Block() as block:
        @block.sync
        def _(sp):
            def state_away(h):
                readout(sp, h, f"su{NT - 1}")
                sp.dma_start(p_delta[0, 0, h], S[:, 0, :]).then_inc(s_out, 16)
            for b in range(3 * HB):
                h, i = b // 3, b % 3
                ring.load(sp, B1 + b + 1)
                if i == 1 and h >= 2:
                    state_away(h - 2)
            state_away(HB - 2)
            ring.load(sp, B2 + RING)
            state_away(HB - 1)
            sp.wait_ge(s_out, 16 * HB)

        @block.tensor
        def _(pe):
            def unit(h, j, k):
                i, part_ = j // 3, j % 3
                b = 3 * h + i
                if k in (None, 0):
                    if part_ == 0:
                        ring.wait(pe, B1 + b)
                    after(pe, pr_, NPB * h + j - 2)
                for kk in (range(KD) if k is None else (k,)):
                    rhs = hT[:, kk, part_ * 512:(part_ + 1) * 512] if part_ < 2 else hT[:, kk, SEQ:TOK]
                    m = nc.tensor.matmul(bank[part_][:, 0:rhs.shape[1]], ring.slots[:, (B1 + b) % RING, kk, :], rhs,
                                         start=kk == 0, stop=kk == KD - 1)
                if kk == KD - 1:
                    m.then_inc(pd if part_ < 2 else ring.used, 1)

            def beside(h, name):
                if h + 1 < HB:
                    for j, k in at_slot[name]:
                        unit(h + 1, j, k)

            def to(h, name, mms):
                n = place[(h, name)]
                if n >= NWB:
                    who, v = read_at[n - NWB]
                    pe.wait_ge(reads[who], v)
                for c, w, l, r in mms:
                    o = bank[3 + n % NWB][:, c:c + w]
                    if r is None:
                        m = nc.tensor.transpose(o, l, ident)
                    else:
                        m = nc.tensor.matmul(o, l, r, start=True, stop=True)
                m.then_inc(wk, 1)

            def tail(h):
                pe.wait_ge(onm, h + 1)
                for gr in range(2):
                    to(h, f"ot{gr}", [(P * (c % 4), P, o_sb[:, c, :], None) for c in range(*GR[gr])])

            for j, k in units:
                unit(0, j, k)
            for h in range(HB):
                q, k_, v = (qkvT[:, h % 2, i, :] for i in range(3))
                ch = lambda t, c: t[:, c * P:(c + 1) * P]
                each = lambda gr, f: [(P * (c % 4), P) + f(c) for c in range(*GR[gr])]
                pe.wait_ge(sqd, 2 * (h + 1))
                to(h, "ss", [(8 * i + c, 1, (M, X)[i][:, c, :], mats[:, M_ONE, 0:1]) for i in range(2) for c in range(NT)])
                beside(h, "ss")
                pe.wait_ge(hdv, 3 * h + 2)
                pe.wait_ge(sild, 3 * (h + 1))
                for gr in range(2):
                    to(h, f"rl{gr}", each(gr, lambda c: (hd[:, h % 2, RW, c:c + 1].to_broadcast([P, P]), None)))
                    to(h, f"ra{gr}", each(gr, lambda c: (gc[:, col(c, h)].to_broadcast([P, P]), None)))
                    to(h, f"kt{gr}", each(gr, lambda c: (ch(k_, c), None)))
                    to(h, f"vt{gr}", each(gr, lambda c: (ch(v, c), None)))
                    to(h, f"kk{gr}", each(gr, lambda c: (ch(k_, c), ch(k_, c))))
                    to(h, f"qk{gr}", each(gr, lambda c: (ch(k_, c), ch(q, c))))
                beside(h, "prep")
                for gr in range(2):
                    pe.wait_ge(mt0, 2 * h + gr + 1)
                    to(h, f"m{gr}", each(gr, lambda c: (MT[:, c, :], None)))
                beside(h, "m")
                for k in range(1, LEVELS):
                    for gr in range(2):
                        readout(pe, h, f"m{gr}" if k == 1 else f"z{k - 1}{gr}")
                        to(h, f"x{k}{gr}", each(gr, lambda c: (LT[:, c, :], M[:, c, :])))
                    beside(h, f"l{k}a")
                    for gr in range(2):
                        readout(pe, h, f"x{k}{gr}")
                        to(h, f"zt{k}{gr}", each(gr, lambda c: (X[:, c, :], MT[:, c, :])))
                        if k < LEVELS - 1:
                            to(h, f"z{k}{gr}", each(gr, lambda c: (MT[:, c, :], X[:, c, :])))
                    beside(h, f"l{k}b")
                if h:
                    tail(h - 1)
                readout(pe, h, f"zt{LEVELS - 1}1")
                for c in range(NT):
                    if c:
                        readout(pe, h, f"su{c - 1}")
                    else:
                        pe.wait_ge(szero, h + 1)
                    to(h, f"ks{c}", [(0, P, ch(k_, c), S[:, c % 2, :])])
                    to(h, f"qs{c}", [(0, P, ch(q, c), S[:, c % 2, :])])
                    beside(h, f"r{c}a")
                    readout(pe, h, f"ks{c}")
                    to(h, f"tr{c}", [(0, P, MT[:, c, :], r_sb[:, c % 2, :])])
                    beside(h, f"r{c}b")
                    readout(pe, h, f"tr{c}")
                    to(h, f"av{c}", [(0, P, AT[:, c, :], vn[:, c % 2, :])])
                    to(h, f"su{c}", [(0, P, kdec[:, c, :], vn[:, c % 2, :])])
                    beside(h, f"r{c}c")
            tail(HB - 1)

        @block.scalar
        def _(act):
            def piece(h, j):
                i, part_ = j // 3, j % 3
                b = 3 * h + i
                if j == 0:
                    after(act, cvd, 3 * h)
                    after(act, tails, 3 * h)
                if part_ < 2:
                    act.wait_ge(pd, 2 * b + part_ + 1)
                    nc.scalar.copy(xpad[:, i, 3 + part_ * 512:3 + (part_ + 1) * 512], bank[part_][:, :]).then_inc(pr_, 1)
                else:
                    act.wait_ge(ring.used, B1 + b + 1)
                    nc.scalar.copy(xpad_s[:, i, :].rearrange("p (b w) -> p b w", w=7)[:, :, 3:7],
                                   bank[2][:, 0:NS].rearrange("p (b t) -> p b t", t=DT)).then_inc(pr_, 1)

            def pieces(h, name):
                if h + 1 < HB:
                    for j in ended[name]:
                        piece(h + 1, j)

            def silu(h, i):
                act.wait_ge(cvd, 3 * h + i + 1)
                nc.scalar.activation(sd[:, i, h * NS:(h + 1) * NS], sd[:, i, h * NS:(h + 1) * NS], ACT.Silu)
                nc.scalar.activation(qkvT[:, h % 2, i, :], qkvT[:, h % 2, i, :], ACT.Silu).then_inc(sild, 1)

            def squares(h, c):
                readout(act, h, f"av{c}")
                nc.scalar.activation(LT[:, c, :], o_sb[:, c, :], ACT.Square, scale=hd[:, h % 2, RQ, c:c + 1],
                                     accum_out=hd[:, h % 2, SO, c:c + 1]).then_inc(sqo, 1)

            for j in range(NPB):
                piece(0, j)
            for i in range(3):
                silu(0, i)
            for h in range(HB):
                more = h + 1 < HB
                w = hd[:, h % 2]
                b = left(act, h, "ss")
                nc.scalar.activation(w[:, RQ:RQ + 2, :], b[:, 0:16].rearrange("p (a b) -> p a b", a=2), ACT.Sqrt,
                                     bias=epsc).then_inc(rd_act, 1)
                act.wait_ge(hdv, 3 * h + 1)
                nc.scalar.activation(w[:, LK, :], w[:, RK, :], ACT.Ln).then_inc(hda, 1)
                pieces(h, "ss")
                for gr in range(2):
                    for name, buf in (("rl", LT), ("ra", AT)):
                        readout(act, h, f"{name}{gr}")
                        for c in range(*GR[gr]):
                            i = nc.scalar.activation(buf[:, c, :], buf[:, c, :], ACT.Exp, bias=w[:, BI, c:c + 1])
                        i.then_inc(exd, 1)
                pieces(h, "prep")
                for gr in range(2):
                    b = left(act, h, f"m{gr}")
                    nc.scalar.copy(flat(M[:, GR[gr][0]:GR[gr][1], :]), b[:, :]).then_inc(rd_act, 1)
                for name in ["m"] + [f"l{k}{x}" for k in range(1, LEVELS) for x in "ab"]:
                    pieces(h, name)
                act.wait_ge(hdv, 3 * h + 3)
                for c in range(NT):
                    b = left(act, h, f"qs{c}")
                    nc.scalar.activation(t1[:, c % 2, :], b[:, 0:P], ACT.Copy, scale=eg[:, col(c, h)]).then_inc(rd_act, 1)
                    pieces(h, f"r{c}a")
                    b = left(act, h, f"tr{c}")
                    nc.scalar.copy(vn[:, c % 2, :], b[:, 0:P]).then_inc(rd_act, 1)
                    pieces(h, f"r{c}b")
                    pieces(h, f"r{c}c")
                    if c:
                        squares(h, c - 1)
                    if more and c in silu_at:
                        silu(h + 1, silu_at[c])
                squares(h, NT - 1)
                act.wait_ge(sqo, NT * (h + 1))
                nc.scalar.activation(w[:, SO, :], w[:, SO, :], ACT.Sqrt, scale=1.0 / E, bias=epsc).then_inc(sqrt_o, 1)

        @block.vector
        def _(dve):
            own = Chain(nc, dve, "b_dve")

            def conv(h, i, steps=range(CW)):
                dve.wait_ge(pr_, NPB * h + 3 * i + 3)
                dve.wait_ge(prefix, 3 * h + i + 1)
                cw = lambda w: cwT[:, w, i * HB + h:i * HB + h + 1]
                xs = xpad_s[:, i, :].rearrange("p (b w) -> p b w", w=7)
                ds = sd[:, i, h * NS:(h + 1) * NS].rearrange("p (b t) -> p b t", t=DT)
                dp = qkvT[:, h % 2, i, :]
                for w in steps:
                    for src, dst, last in ((xs[:, :, w:w + DT], ds, False), (xpad[:, i, w:w + SEQ], dp, True)):
                        if w == 0:
                            x = nc.vector.tensor_scalar(dst, src, cw(0), None, ALU.mult)
                        else:
                            x = nc.vector.scalar_tensor_tensor(out=dst, in0=src, scalar=cw(w), in1=dst,
                                                               op0=ALU.mult, op1=ALU.add)
                        if last and w == CW - 1:
                            x.then_inc(cvd, 1)
                        else:
                            conv_step(x)

            stepped = [0]

            def conv_step(x):
                stepped[0] += 1
                x.then_inc(cstep, 1)

            def conv_ready():
                after(dve, cstep, stepped[0])

            for i in range(3):
                for w in range(CW):
                    conv_ready()
                    conv(0, i, (w,))
            wide4 = lambda v: v.unsqueeze(1).to_broadcast([P, 4, P])
            bk = lambda b: b[:, :].rearrange("p (c i) -> p c i", i=P)

            def ot(h):
                for gr in range(2):
                    b = left(dve, h, f"ot{gr}")
                    nc.vector.tensor_scalar(brT[:, h, gr * 512:(gr + 1) * 512], b[:, :], onw, None,
                                            ALU.mult).then_inc(rd_dve, 1)

            for h in range(HB):
                w = hd[:, h % 2]
                g = lambda v: hcols(v, h)
                readout(dve, h, "ss")
                nc.vector.reciprocal(w[:, RQ:RQ + 2, :], w[:, RQ:RQ + 2, :]).then_inc(hdv, 1)
                dve.wait_ge(hda, h + 1)
                dve.wait_ge(hdv, 3 * h + 1)
                own(nc.vector.tensor_tensor(w[:, BI, :], w[:, LK, :], g(gc), ALU.subtract))
                own(nc.vector.tensor_tensor(w[:, RW, :], w[:, LK, :], g(gc), ALU.add))
                nc.vector.tensor_tensor(w[:, RW, :], w[:, RW, :], g(lbeta), ALU.add).then_inc(hdv, 1)
                own(nc.vector.tensor_tensor(w[:, KD_, :], w[:, RK, :], g(ekd), ALU.mult))
                own(nc.vector.tensor_tensor(w[:, NC_, :], w[:, RK, :], g(beta), ALU.mult))
                own(nc.vector.scalar_tensor_tensor(out=w[:, NC_, :], in0=w[:, NC_, :], scalar=-1.0, in1=g(eg),
                                                   op0=ALU.mult, op1=ALU.mult))
                nc.vector.tensor_scalar(w[:, RQ, :], w[:, RQ, :], SCALE, None, ALU.mult).then_inc(hdv, 1)
                for gr in range(2):
                    cs = slice(*GR[gr])
                    for name, buf, m in (("rl", LT, M_GT), ("ra", AT, M_GE)):
                        b = left(dve, h, f"{name}{gr}")
                        nc.vector.tensor_tensor(buf[:, cs, :], bk(b), wide4(mat(m)), ALU.add).then_inc(rd_dve, 1)
                    for name, buf, f in (("kt", kdec, w[:, KD_, cs]), ("vt", vb, g(beta)[:, cs])):
                        b = left(dve, h, f"{name}{gr}")
                        nc.vector.tensor_tensor(buf[:, cs, :], bk(b), f.unsqueeze(2).to_broadcast([P, 4, P]),
                                                ALU.mult).then_inc(rd_dve, 1)
                    for t, (name, buf) in enumerate((("kk", LT), ("qk", AT))):
                        dve.wait_ge(exd, 4 * h + 2 * gr + t + 1)
                        b = left(dve, h, f"{name}{gr}")
                        nc.vector.tensor_tensor(buf[:, cs, :], buf[:, cs, :], bk(b), ALU.mult).then_inc(rd_dve, 1)
                for gr in range(2):
                    cs = slice(*GR[gr])
                    readout(dve, h, f"kk{gr}")
                    own(nc.vector.tensor_tensor(MT[:, cs, :], LT[:, cs, :], wide4(mat(M_LEV)), ALU.mult))
                    nc.vector.tensor_tensor(MT[:, cs, :], wide4(ident), MT[:, cs, :], ALU.subtract).then_inc(mt0, 1)
                for k in range(1, LEVELS):
                    for gr in range(2):
                        b = left(dve, h, f"x{k}{gr}")
                        nc.vector.tensor_tensor(X[:, slice(*GR[gr]), :], bk(b), wide4(mat(M_LEV + k)),
                                                ALU.mult).then_inc(rd_dve, 1)
                    for gr in range(2):
                        for name, buf in (("zt", MT), ("z", M))[:2 if k < LEVELS - 1 else 1]:
                            if k < LEVELS - 1:
                                left(dve, h, f"z{k}{gr}")
                            b = left(dve, h, f"{name}{k}{gr}")
                            v = buf[:, slice(*GR[gr]), :]
                            nc.vector.tensor_tensor(v, v, bk(b), ALU.subtract).then_inc(rd_dve, 1)
                if h:
                    ot(h - 1)
                for c in range(NT):
                    b = left(dve, h, f"ks{c}")
                    nc.vector.scalar_tensor_tensor(out=r_sb[:, c % 2, :], in0=b[:, 0:P], scalar=w[:, NC_, c:c + 1],
                                                   in1=vb[:, c, :], op0=ALU.mult, op1=ALU.add).then_inc(rd_dve, 1)
                    half = 2 * (c in (1, 4, 7))
                    if h + 1 < HB and c in conv_at:
                        conv_ready()
                        conv(h + 1, conv_at[c], (half,))
                    b = left(dve, h, f"av{c}")
                    readout(dve, h, f"qs{c}")
                    nc.vector.tensor_tensor(o_sb[:, c, :], b[:, 0:P], t1[:, c % 2, :], ALU.add).then_inc(rd_dve, 1)
                    b = left(dve, h, f"su{c}")
                    nc.vector.scalar_tensor_tensor(out=S[:, (c + 1) % 2, :], in0=S[:, c % 2, :], scalar=egl[:, col(c, h)],
                                                   in1=b[:, 0:P], op0=ALU.mult, op1=ALU.add).then_inc(rd_dve, 1)
                    if h + 1 < HB and c in conv_at:
                        conv_ready()
                        conv(h + 1, conv_at[c], (half + 1,))
                dve.wait_ge(sqrt_o, h + 1)
                own(nc.vector.reciprocal(w[:, SO, :], w[:, SO, :]))
                nc.vector.tensor_tensor(w[:, SO, :], w[:, SO, :], w[:, RQ, :], ALU.mult).then_inc(fac, 1)
            ot(HB - 1)

        @block.gpsimd
        def _(pool):
            own = Chain(nc, pool, "b_pool")
            def prefixes(h):
                for i in range(3):
                    nc.gpsimd.tensor_copy(xpad_s[:, i, :].rearrange("p (b w) -> p b w", w=7)[:, :, 0:3],
                                          cst[:, i * HB + h, :].rearrange("p (b w) -> p b w", w=3)).then_inc(prefix, 1)

            def prepare(h):
                for i in range(3):
                    b = i * HB + h
                    pool.wait_ge(pr_, NPB * h + 3 * i + 3)
                    nc.gpsimd.tensor_copy(nconv[:, b, 0:3], xpad[:, i, SEQ:SEQ + 3])
                    nc.gpsimd.tensor_copy(nconv[:, b, 3:27].rearrange("p (b w) -> p b w", w=3),
                                          xpad_s[:, i, :].rearrange("p (b w) -> p b w", w=7)[:, :, 4:7]).then_inc(tails, 1)
                    if i < 2:
                        pool.wait_ge(sild, 3 * h + i + 1)
                        if h and not i:
                            readout(pool, h - 1, f"zt{LEVELS - 1}1")
                        x = qkvT[:, h % 2, i, :].rearrange("p (c t) -> p c t", t=P)
                        nc.gpsimd.tensor_tensor((M, X)[i][:, :, :], x, x, ALU.mult).then_inc(sqd, 1)

            own(nc.gpsimd.memset(xpad[:, :, 0:CW - 1], 0.0))
            copy_cache(pool, ck2, sk2, 512, 0)
            copy_cache(pool, cv2, sv2, 512, 0)
            prefixes(0)
            prepare(0)
            for h in range(HB):
                after(pool, s_out, 16 * h)
                nc.gpsimd.memset(S[:, 0, :], 0.0).then_inc(szero, 1)
                if h + 1 < HB:
                    pool.wait_ge(cvd, 3 * (h + 1))
                    prefixes(h + 1)
                    prepare(h + 1)
                pool.wait_ge(fac, h + 1)
                nc.gpsimd.tensor_tensor(o_sb[:, :, :], o_sb[:, :, :],
                                        hd[:, h % 2, SO, :].unsqueeze(2).to_broadcast([P, NT, P]), ALU.mult).then_inc(onm, 1)

    phase_over()

    at[0] = rbase
    mq = take(2, TOK)
    zm = take(2, TOK)
    zo = take(2, 2, TOK)
    sS2, pr2, pT2 = take(2, 256), take(2, 256), take(2, 256)
    conv_rows = take(24, P)[0:27]
    st2 = take(24)
    (p2, pr2d, sc2, scr2, mx2, ex2, nm2, tn2, tr2, pv2, or2, zo2, nct, ncr) = (sem(f"m_{n}") for n in (
        "piece_done", "piece_read", "scores", "scores_read", "max", "exp", "normed", "turned", "turned_read",
        "values", "values_read", "gated", "conv_turned", "conv_read"))
    nco = stored["conv"]
    NP2 = 12
    beside = lambda u: range(u + u // 2, u + 1 + (u + 1) // 2)

    with nc.Block() as block:
        @block.sync
        def _(sp):
            ring.load(sp, B2 + 4 * H)
            sp.wait_ge(ncr, 6)
            sp.dma_start(p_conv[0, 0].rearrange("w (b p) -> w b p", p=P), conv_rows[0:3]).then_inc(nco, 16)
            sp.dma_start(s_conv[0].rearrange("b w (k p) -> (b w) k p", p=P), conv_rows[3:27]).then_inc(nco, 16)
            sp.wait_ge(nco, 32)

        @block.tensor
        def _(pe):
            def piece(s, j):
                i, part_ = j // 3, j % 3
                b = 4 * s + i
                if part_ == 0:
                    ring.wait(pe, B2 + b)
                after(pe, pr2d, 3 * b + part_ - 2)
                for k in range(KD):
                    rhs = hT[:, k, part_ * 512:(part_ + 1) * 512] if part_ < 2 else hT[:, k, SEQ:TOK]
                    m = nc.tensor.matmul(bank[part_][:, 0:rhs.shape[1]], ring.slots[:, (B2 + b) % RING, k, :], rhs,
                                         start=k == 0, stop=k == KD - 1)
                m.then_inc(p2 if part_ < 2 else ring.used, 1)

            def turn_probs(s, u):
                x = 8 * s + u
                pe.wait_ge(nm2, x + 1)
                after(pe, tr2, x - 1)
                for c in range(2):
                    m = nc.tensor.transpose(bank[5 + x % 2][:, c * P:(c + 1) * P], pr2[:, x % 2, c * P:(c + 1) * P], ident)
                m.then_inc(tn2, 1)

            def values(s, u):
                x = 8 * s + u
                pe.wait_ge(tr2, x + 1)
                after(pe, or2, x)
                for c in range(2):
                    m = nc.tensor.matmul(bank[7][:, 0:P], mv[:, 2 + c, s * E:(s + 1) * E], pT2[:, x % 2, c * P:(c + 1) * P],
                                         start=c == 0, stop=c == 1)
                m.then_inc(pv2, 1)

            for j in range(NP2):
                piece(0, j)
            for t in range(6):
                after(pe, ncr, t - 1)
                for b in range(4):
                    m = nc.tensor.transpose(bank[5 + t % 2][0:27, b * P:(b + 1) * P], nconv[:, 4 * t + b, :], ident)
                m.then_inc(nct, 1)
            pe.wait_ge(ncr, 6)
            for s in range(H):
                more = s + 1 < H
                pe.wait_ge(pr2d, NP2 * (s + 1))
                for u in range(8):
                    x = 8 * s + u
                    after(pe, scr2, x - 1)
                    nc.tensor.matmul(bank[3 + x % 2][:, 0:256], mq[:, s % 2, u * P:(u + 1) * P], mkT[:, H + s, :],
                                     start=True, stop=True).then_inc(sc2, 1)
                    if u:
                        turn_probs(s, u - 1)
                    if more:
                        for j in beside(u):
                            piece(s + 1, j)
                    if u:
                        values(s, u - 1)
                turn_probs(s, 7)
                values(s, 7)

        @block.scalar
        def _(act):
            def piece(s, j):
                i, part_ = j // 3, j % 3
                b = 4 * s + i
                src = bank[part_][:, 0:512 if part_ < 2 else NS]
                if part_ < 2:
                    act.wait_ge(p2, 2 * b + part_ + 1)
                else:
                    act.wait_ge(ring.used, B2 + b + 1)
                cs = slice(part_ * 512, (part_ + 1) * 512)
                if i == 0:
                    if part_ == 0:
                        after(act, or2, 8 * (s - 1))
                    dst = mq[:, s % 2, cs] if part_ < 2 else qms[:, s * NS:(s + 1) * NS]
                elif i == 1:
                    dst = zm[:, s % 2, cs] if part_ < 2 else zs[:, HB + s, :]
                else:
                    if part_ == 0:
                        after(act, zo2, 2 * (s - 2) + i - 1)
                    dst = zo[:, s % 2, i - 2, cs] if part_ < 2 else zs[:, 2 * s + i - 2, :]
                nc.scalar.activation(dst, src, ACT.Silu if i else ACT.Copy).then_inc(pr2d, 1)

            for j in range(NP2):
                piece(0, j)
            for s in range(H):
                more = s + 1 < H
                for u in range(8):
                    x = 8 * s + u
                    act.wait_ge(mx2, x + 1)
                    after(act, pv2, x - 1)
                    nc.scalar.activation(pr2[:, x % 2, :], sS2[:, x % 2, :], ACT.Exp, bias=st2[:, u:u + 1],
                                         accum_out=st2[:, 8 + u:9 + u]).then_inc(ex2, 1)
                    if more:
                        for j in beside(u):
                            piece(s + 1, j)

        @block.vector
        def _(dve):
            own = Chain(nc, dve, "m_dve")
            for t in range(6):
                dve.wait_ge(nct, t + 1)
                nc.vector.tensor_copy(conv_rows[:, 4 * t:4 * t + 4, :].rearrange("p a b -> p (a b)"),
                                      bank[5 + t % 2][0:27, :]).then_inc(ncr, 1)

            def normed(s, u):
                x = 8 * s + u
                dve.wait_ge(ex2, x + 1)
                own(nc.vector.reciprocal(st2[:, 16 + u:17 + u], st2[:, 8 + u:9 + u]))
                nc.vector.tensor_scalar(pr2[:, x % 2, :], pr2[:, x % 2, :], st2[:, 16 + u:17 + u], None,
                                        ALU.mult).then_inc(nm2, 1)

            def turned(s, u):
                x = 8 * s + u
                dve.wait_ge(tn2, x + 1)
                nc.vector.tensor_copy(pT2[:, x % 2, :], bank[5 + x % 2][:, 0:256]).then_inc(tr2, 1)

            def outputs(s, u):
                x = 8 * s + u
                dve.wait_ge(pv2, x + 1)
                nc.vector.tensor_tensor(brT[:, HB + s, u * P:(u + 1) * P], bank[7][:, 0:P],
                                        zm[:, s % 2, u * P:(u + 1) * P], ALU.mult).then_inc(or2, 1)

            for s in range(H):
                dve.wait_ge(pr2d, NP2 * s + 6)
                for u in range(8):
                    x = 8 * s + u
                    dve.wait_ge(sc2, x + 1)
                    after(dve, ex2, x - 1)
                    nc.vector.tensor_scalar(sS2[:, x % 2, :], bank[3 + x % 2][:, 0:256], SCALE, None,
                                            ALU.mult).then_inc(scr2, 1)
                    dve.wait_ge(scr2, x + 1)
                    nc.vector.reduce_max(st2[:, u:u + 1], sS2[:, x % 2, :], axis=AX, negate=True).then_inc(mx2, 1)
                    if u:
                        turned(s, u - 1)
                    normed(s, u)
                    if u:
                        outputs(s, u - 1)
                turned(s, 7)
                outputs(s, 7)

        @block.gpsimd
        def _(pool):
            for s in range(H):
                for i in range(2):
                    pool.wait_ge(pr2d, NP2 * s + 3 * (i + 3))
                    v = brT[:, 2 * s + i, 0:SEQ]
                    nc.gpsimd.tensor_tensor(v, v, zo[:, s % 2, i, 0:SEQ], ALU.mult).then_inc(zo2, 1)

    phase_over()

    at[0] = rbase
    sq = take(2, 256)
    kdec_s, vb_s = take(2, P), take(2, P)
    LTs, ATs, Ms, MTs, Xs, rs, vns, os_, t1s, KSr = (take(2, P) for _ in range(10))
    kqs = take(2, 2, P)
    sw = take(2, 10)
    stq = take(3, 4, P)
    snew = take(2, 4, P)
    vex = take(2, 4, P)
    assert at[0] <= rbase + 3 * (SEQ + 3) + 3 * 56 + 6 * SEQ + 6 * NT * P
    NQ = 2 * 32 // 4
    ld3 = [sem(f"d_states_in{i}") for i in range(3)]
    (dsq, dpe, ddv, dac, du, dks, dsu, dsv, dvx) = (sem(f"d_{n}") for n in (
        "squares", "pe", "dve", "act", "unit", "state_products", "update", "updated", "expanded"))
    dso = (stored["sample_states0"], stored["sample_states1"])

    def quad(q):
        h, b = q // 2, 4 * (q % 2)
        return h // 4, h, b

    with nc.Block() as block:
        @block.sync
        def _(sp):
            for n in range(2 * NQ):
                q = n % NQ
                t, h, b = quad(q)
                if n >= 3:
                    m = n - 3
                    sp.wait_ge(dks if m < NQ else dsv, m + 1 if m < NQ else m - NQ + 1)
                sp.dma_start(stq[:, n % 3], state_delta[0, b:b + 4, h].rearrange("b k v -> k b v")).then_inc(ld3[n % 3], 16)
                if n >= NQ + 1:
                    m = n - NQ - 1
                    t, h, b = quad(m)
                    sp.wait_ge(dsv, m + 1)
                    sp.dma_start(s_delta[0, b:b + 4, h].rearrange("b k v -> k b v"), snew[:, m % 2]).then_inc(dso[m % 2], 16)
            t, h, b = quad(NQ - 1)
            sp.wait_ge(dsv, NQ)
            sp.dma_start(s_delta[0, b:b + 4, h].rearrange("b k v -> k b v"), snew[:, (NQ - 1) % 2]).then_inc(dso[(NQ - 1) % 2], 16)
            for d in dso:
                sp.wait_ge(d, 16 * NQ // 2)

        tl = lambda v, t: v[:, t * P:(t + 1) * P]

        @block.tensor
        def _(pe):
            pe.wait_ge(dsq, 2)
            for i in range(2):
                for t in range(2):
                    m = nc.tensor.matmul(bank[0][:, 2 * i + t:2 * i + t + 1], tl(sq[:, i, :], t), mats[:, M_ONE, 0:1],
                                         start=True, stop=True)
            m.then_inc(dpe, 1)
            for t in range(2):
                nc.tensor.transpose(bank[1][:, t * P:(t + 1) * P], tl(sd[:, 1, :], t), ident)
                nc.tensor.transpose(bank[1][:, 256 + t * P:256 + (t + 1) * P], tl(sd[:, 2, :], t), ident)
            for t in range(2):
                nc.tensor.matmul(bank[2][:, t * P:(t + 1) * P], tl(sd[:, 1, :], t), tl(sd[:, 1, :], t), start=True, stop=True)
                m = nc.tensor.matmul(bank[2][:, 256 + t * P:256 + (t + 1) * P], tl(sd[:, 1, :], t), tl(sd[:, 0, :], t),
                                     start=True, stop=True)
            m.then_inc(dpe, 1)
            for q in range(NQ):
                t, h, b = quad(q)
                pe.wait_ge(ld3[q % 3], 16 * (q // 3 + 1))
                for u in range(4):
                    o = (h % 4) * NS + (b + u) * DT
                    for i in range(2):
                        m = nc.tensor.matmul(bank[3][:, i * 256 + t * P + o:i * 256 + t * P + o + DT], stq[:, q % 3, u, :],
                                             tl(sd[:, 1 - i, :], t)[:, o:o + DT], start=True, stop=True)
                m.then_inc(dks, 1)
            pe.wait_ge(ddv, 1)
            for t in range(2):
                nc.tensor.transpose(bank[4][:, t * P:(t + 1) * P], sw[:, t, 6:7].to_broadcast([P, P]), ident)
                m = nc.tensor.transpose(bank[4][:, 256 + t * P:256 + (t + 1) * P], gc[:, 64 + t:65 + t].to_broadcast([P, P]),
                                        ident)
            m.then_inc(dpe, 1)
            pe.wait_ge(ddv, 2)
            for t in range(2):
                for i in range(2):
                    m = nc.tensor.transpose(bank[5][:, i * 256 + t * P:i * 256 + (t + 1) * P], kqs[:, i, t, :], ident)
            m.then_inc(dpe, 1)
            pe.wait_ge(ddv, 3)
            for t in range(2):
                m = nc.tensor.transpose(bank[6][:, t * P:(t + 1) * P], MTs[:, t, :], ident)
            m.then_inc(dpe, 1)
            pe.wait_ge(dac, 3)
            for t in range(2):
                m = nc.tensor.matmul(bank[7][:, t * P:(t + 1) * P], LTs[:, t, :], Ms[:, t, :], start=True, stop=True)
            m.then_inc(dpe, 1)
            pe.wait_ge(ddv, 4)
            for t in range(2):
                m = nc.tensor.matmul(bank[0][:, t * P:(t + 1) * P], Xs[:, t, :], MTs[:, t, :], start=True, stop=True)
            m.then_inc(dpe, 1)
            pe.wait_ge(ddv, 6)
            for t in range(2):
                m = nc.tensor.matmul(bank[1][:, t * P:(t + 1) * P], MTs[:, t, :], rs[:, t, :], start=True, stop=True)
            m.then_inc(dpe, 1)
            pe.wait_ge(dac, 4)
            for t in range(2):
                m = nc.tensor.matmul(bank[2][:, t * P:(t + 1) * P], ATs[:, t, :], vns[:, t, :], start=True, stop=True)
            m.then_inc(dpe, 1)
            for q in range(NQ):
                t, h, b = quad(q)
                pe.wait_ge(dvx, q + 1)
                after(pe, dsv, q - 1)
                nc.tensor.matmul(bank[6 + q % 2][:, :], kdec_s[:, t, :], vex[:, q % 2].rearrange("p a b -> p (a b)"),
                                 start=True, stop=True).then_inc(dsu, 1)
            pe.wait_ge(ddv, 8)
            for t in range(2):
                m = nc.tensor.transpose(bank[3][:, t * P:(t + 1) * P], os_[:, t, :], ident)
            m.then_inc(dpe, 1)

        @block.scalar
        def _(act):
            own = Chain(nc, act, "d_act_own")
            act.wait_ge(dpe, 1)
            nc.scalar.activation(sw[:, :, 0:2], bank[0][:, 0:4].rearrange("p (i t) -> p t i", i=2), ACT.Sqrt,
                                 bias=epsc).then_inc(dac, 1)
            act.wait_ge(du, 1)
            nc.scalar.activation(sw[:, :, 2:3], sw[:, :, 1:2], ACT.Ln).then_inc(dac, 1)
            act.wait_ge(du, 2)
            for t in range(2):
                nc.scalar.activation(LTs[:, t, :], LTs[:, t, :], ACT.Exp, bias=sw[:, t, 5:6])
                m = nc.scalar.activation(ATs[:, t, :], ATs[:, t, :], ACT.Exp, bias=sw[:, t, 5:6])
            m.then_inc(du, 1)
            act.wait_ge(dpe, 5)
            nc.scalar.copy(flat(Ms), bank[6][:, 0:256]).then_inc(dac, 1)
            act.wait_ge(dpe, 8)
            nc.scalar.copy(flat(vns), bank[1][:, 0:256]).then_inc(dac, 1)
            act.wait_ge(ddv, 7)
            for t in range(2):
                m = nc.scalar.activation(t1s[:, t, :], os_[:, t, :], ACT.Square, scale=sw[:, t, 0:1],
                                         accum_out=sw[:, t, 7:8])
            own(m)
            nc.scalar.activation(sw[:, :, 7:8], sw[:, :, 7:8], ACT.Sqrt, scale=1.0 / E, bias=epsc).then_inc(dac, 1)

        @block.vector
        def _(dve):
            own = Chain(nc, dve, "d_dve_own")
            gt2 = lambda v: v[:, 64:66].unsqueeze(2)
            rows2 = lambda b, o: b[:, o:o + 256].rearrange("p (t i) -> p t i", t=2)
            wide2 = lambda m: mat(m).unsqueeze(1).to_broadcast([P, 2, P])
            for i in range(2):
                nc.vector.tensor_tensor(sq[:, i, :], sd[:, i, :], sd[:, i, :], ALU.mult).then_inc(dsq, 1)
            dve.wait_ge(dac, 1)
            nc.vector.reciprocal(sw[:, :, 0:2], sw[:, :, 0:2]).then_inc(du, 1)
            dve.wait_ge(dac, 2)
            dve.wait_ge(du, 1)
            own(nc.vector.tensor_tensor(sw[:, :, 5:6], sw[:, :, 2:3], gt2(gc), ALU.subtract))
            own(nc.vector.tensor_tensor(sw[:, :, 6:7], sw[:, :, 2:3], gt2(gc), ALU.add))
            nc.vector.tensor_tensor(sw[:, :, 6:7], sw[:, :, 6:7], gt2(lbeta), ALU.add).then_inc(ddv, 1)
            own(nc.vector.tensor_tensor(sw[:, :, 3:4], sw[:, :, 1:2], gt2(ekd), ALU.mult))
            own(nc.vector.tensor_tensor(sw[:, :, 4:5], sw[:, :, 1:2], gt2(beta), ALU.mult))
            own(nc.vector.scalar_tensor_tensor(out=sw[:, :, 4:5], in0=sw[:, :, 4:5], scalar=-1.0, in1=gt2(eg),
                                               op0=ALU.mult, op1=ALU.mult))
            own(nc.vector.tensor_scalar(sw[:, :, 0:1], sw[:, :, 0:1], SCALE, None, ALU.mult))
            dve.wait_ge(dks, NQ)
            nc.vector.tensor_copy(kqs[:, :, :, :].rearrange("p a b c -> p (a b c)"), bank[3][:, :]).then_inc(ddv, 1)
            dve.wait_ge(dpe, 3)
            own(nc.vector.tensor_tensor(LTs[:, :, :], rows2(bank[4], 0), wide2(M_SGT), ALU.add))
            nc.vector.tensor_tensor(ATs[:, :, :], rows2(bank[4], 256), wide2(M_SGE), ALU.add).then_inc(du, 1)
            own(nc.vector.tensor_tensor(kdec_s[:, :, :], rows2(bank[1], 0), sw[:, :, 3:4].to_broadcast([P, 2, P]), ALU.mult))
            own(nc.vector.tensor_tensor(vb_s[:, :, :], rows2(bank[1], 256), gt2(beta).to_broadcast([P, 2, P]), ALU.mult))
            dve.wait_ge(du, 3)
            own(nc.vector.tensor_tensor(LTs[:, :, :], LTs[:, :, :], rows2(bank[2], 0), ALU.mult))
            own(nc.vector.tensor_tensor(ATs[:, :, :], ATs[:, :, :], rows2(bank[2], 256), ALU.mult))
            own(nc.vector.tensor_tensor(MTs[:, :, :], LTs[:, :, :], wide2(M_LEV), ALU.mult))
            nc.vector.tensor_tensor(MTs[:, :, :], wide2(M_ID), MTs[:, :, :], ALU.subtract).then_inc(ddv, 1)
            dve.wait_ge(dpe, 6)
            nc.vector.tensor_tensor(Xs[:, :, :], rows2(bank[7], 0), wide2(M_LEV + 1), ALU.mult).then_inc(ddv, 1)
            dve.wait_ge(dpe, 7)
            nc.vector.tensor_tensor(MTs[:, :, :], MTs[:, :, :], rows2(bank[0], 0), ALU.subtract).then_inc(ddv, 1)
            for t in range(2):
                m = nc.vector.scalar_tensor_tensor(out=rs[:, t, :], in0=bank[5][:, t * P:(t + 1) * P],
                                                   scalar=sw[:, t, 4:5], in1=vb_s[:, t, :], op0=ALU.mult, op1=ALU.add)
            m.then_inc(ddv, 1)
            own(nc.vector.tensor_tensor(KSr[:, :, :], rows2(bank[5], 256), gt2(eg).to_broadcast([P, 2, P]), ALU.mult))
            dve.wait_ge(dpe, 9)
            own(nc.vector.tensor_tensor(os_[:, :, :], rows2(bank[2], 0), KSr[:, :, :], ALU.add))
            nc.vector.tensor_copy(t1s[:, :, 0:1], os_[:, :, 0:1]).then_inc(ddv, 1)
            for q in range(NQ + 1):
                if q < NQ:
                    t, h, b = quad(q)
                    after(dve, dsu, q - 1)
                    u0 = (h % 4) * 8 + b
                    nc.vector.tensor_tensor(vex[:, q % 2], vns[:, t, :].unsqueeze(1).to_broadcast([P, 4, P]),
                                            mats[:, M_HSEL, 32 + u0:36 + u0].unsqueeze(2).to_broadcast([P, 4, P]),
                                            ALU.mult).then_inc(dvx, 1)
                if q:
                    m_ = q - 1
                    t, h, b = quad(m_)
                    n = NQ + m_
                    dve.wait_ge(ld3[n % 3], 16 * (n // 3 + 1))
                    after(dve, dso[m_ % 2], 16 * (m_ // 2))
                    u0 = 32 * t + (h % 4) * 8 + b
                    own(nc.vector.tensor_tensor(snew[:, m_ % 2], stq[:, n % 3],
                                                eglu[:, u0:u0 + 4].unsqueeze(2).to_broadcast([P, 4, P]), ALU.mult))
                    dve.wait_ge(dsu, m_ + 1)
                    nc.vector.tensor_tensor(snew[:, m_ % 2], snew[:, m_ % 2],
                                            bank[6 + m_ % 2][:, :].rearrange("p (a b) -> p a b", a=4),
                                            ALU.add).then_inc(dsv, 1)
            dve.wait_ge(dac, 5)
            own(nc.vector.reciprocal(sw[:, :, 7:8], sw[:, :, 7:8]))
            own(nc.vector.tensor_tensor(sw[:, :, 7:8], sw[:, :, 7:8], sw[:, :, 0:1], ALU.mult))
            nc.vector.tensor_tensor(os_[:, :, :], os_[:, :, :], sw[:, :, 7:8].to_broadcast([P, 2, P]),
                                    ALU.mult).then_inc(ddv, 1)
            dve.wait_ge(dpe, 10)
            dst = brT[:, 0:HB, SEQ:TOK]
            own(nc.vector.tensor_scalar(dst, bank[3][:, 0:256].rearrange("p (h t) -> p h t", h=HB), onw, None, ALU.mult))
            own(nc.vector.tensor_tensor(dst, dst, zs[:, 0:HB, :], ALU.mult))

    phase_over()
    sample_attention("sm1_", mem_sources(cmk, 1), mem_sources(cmv, 1), 2, lambda g: qms, None, HB, False,
                     rbase + 12 * D, (12, w_out_b[0], w_out_in[1]))

    def x1_of(n):
        return x1[n * P:min((n + 1) * P, TOK)]

    out_phase("ob_", 12, w_out_in[1], x1_of, final_w, hT_at, True)

    with nc.Block() as block:
        @block.sync
        def _(sp):
            sp.wait_ge(copies, 16 * NCOPY)


INS = ['x_prompt', 'x_sample', 'cache_win_k0', 'cache_win_v0', 'cache_win_k1', 'cache_win_v1', 'cache_win_k2',
       'cache_win_v2', 'state_conv', 'state_delta', 'cache_mem_k', 'cache_mem_v', 'mem_prompt', 'norm_w',
       'final_norm_w', 'rel_bias', 'w_in_a', 'w_out_a', 'w_in_b', 'conv_w', 'a_log', 'dt_bias', 'o_norm_w',
       'w_out_b', 'w_mem_kv']


def out_shapes():
    pw = [(1, 1, min(w, SEQ), H, E) for w, _ in GROUPS for _ in range(2)]
    sw = [(1, NB, min(w, PAST + DT), H, E) for w, _ in GROUPS for _ in range(2)]
    return ([(1, SEQ, D), (NB, DT, D)] + pw
            + [(1, 1, CW - 1, 3 * WB), (1, 1, HB, E, E), (2, 1, NMEM, H, E), (2, 1, NMEM, H, E)]
            + sw + [(1, NB, CW - 1, 3 * WB), (1, NB, HB, E, E)])


def kernel(**inputs):
    import concourse.bacc as bacc
    from concourse.bass_utils import run_bass_kernel_spmd

    nc = bacc.Bacc("TRN2", target_bir_lowering=False, num_devices=1)
    arrays = {f"in_{n}": np.ascontiguousarray(inputs[n]) for n in INS}
    arrays.update({f"in_{n}": a for n, a in shape_constants().items()})
    ins = [nc.dram_tensor(n, a.shape, mybir.dt.from_np(a.dtype), kind="ExternalInput").ap()
           for n, a in arrays.items()]
    shapes = out_shapes()
    outs = [nc.dram_tensor(f"out_{i}", s, F32, kind="ExternalOutput").ap() for i, s in enumerate(shapes)]
    build(nc, ins, outs)
    r = run_bass_kernel_spmd(nc, [arrays], core_ids=[0])
    return tuple(r.results[0][f"out_{i}"] for i in range(len(shapes)))
```
